# Optimizing a Trainium2 kernel written in Bass

```python
import jax, jax.numpy as jnp
from jax import lax
import numpy as np

D_MODEL = 1024
BATCH = 1
SEQ = 1024
DEPTH = 2

N_MIXERS = 3
POOL_WINDOWS = (2, 4, 8, 16)
POOL_GROUPS = len(POOL_WINDOWS)
POOL_GROUP_DIM = D_MODEL // POOL_GROUPS
SGU_CHUNK = 128
SGU_WIDTH = D_MODEL
SGU_HEAD_DIM = 128
SGU_HEADS = SGU_WIDTH // SGU_HEAD_DIM
MLA_HEADS = 16
MLA_Q_LORA = 256
MLA_KV_LORA = 128
MLA_NOPE = 128
MLA_ROPE = 64
MLA_V = 128
ROPE_THETA = 10000.0
Q_BLOCK = 128
D_FF = 4 * D_MODEL
RMS_EPS = 1e-6
LN_EPS = 1e-5
MAX_POS_OFFSET = 4096
N_POOL_LAYERS = len(range(0, DEPTH, N_MIXERS))
N_SGU_LAYERS = len(range(1, DEPTH, N_MIXERS))
N_MLA_LAYERS = len(range(2, DEPTH, N_MIXERS))


def rmsnorm(x, g):
    xf = x.astype(jnp.float32)
    y = xf * lax.rsqrt(jnp.mean(xf * xf, axis=-1, keepdims=True) + RMS_EPS)
    return (y * g.astype(jnp.float32)).astype(x.dtype)

def layernorm(x, g, b):
    xf = x.astype(jnp.float32)
    mu = jnp.mean(xf, axis=-1, keepdims=True)
    xc = xf - mu
    var = jnp.mean(xc * xc, axis=-1, keepdims=True)
    y = xc * lax.rsqrt(var + LN_EPS)
    return (y * g.astype(jnp.float32) + b.astype(jnp.float32)).astype(x.dtype)

def modulate(h, shift, scale):
    return h * (1.0 + scale[:, None, :]) + shift[:, None, :]

def pool_mixer(h, w, scale):
    B_, S_, _ = h.shape
    hf = h.astype(jnp.float32).reshape(B_, S_, POOL_GROUPS, POOL_GROUP_DIM)
    cs = jnp.cumsum(hf, axis=1)
    cs = jnp.concatenate([jnp.zeros_like(cs[:, :1]), cs], axis=1)
    t = jnp.arange(S_, dtype=jnp.float32)
    outs = []
    for gi, win in enumerate(POOL_WINDOWS):
        csg = cs[:, :, gi]
        upper = csg[:, 1:]
        lower = jnp.concatenate([jnp.zeros_like(csg[:, :win - 1]), csg[:, :S_ - win + 1]], axis=1)
        count = jnp.minimum(t + 1.0, float(win))[None, :, None]
        outs.append((upper - lower) / count - hf[:, :, gi])
    pooled = jnp.stack(outs, axis=2).astype(h.dtype)
    y = jnp.einsum('bsgc,gcd->bsgd', pooled, w).reshape(B_, S_, D_MODEL)
    return y * scale

def sgu_mixer(h, w_in, ln_g, ln_b, w_s, b_s, w_out):
    B_, S_, _ = h.shape
    z = jax.nn.gelu(h @ w_in, approximate=False)
    u, v = jnp.split(z, 2, axis=-1)
    v = layernorm(v, ln_g, ln_b)
    nc = S_ // SGU_CHUNK
    v = v.reshape(B_, nc, SGU_CHUNK, SGU_HEADS, SGU_HEAD_DIM)
    mask = jnp.tril(jnp.ones((SGU_CHUNK, SGU_CHUNK), dtype=bool))
    ws = jnp.where(mask[None], w_s, 0)
    mixed = jnp.einsum('hts,bnshc->bnthc', ws, v) + b_s.T[None, None, :, :, None]
    gated = u * mixed.reshape(B_, S_, SGU_WIDTH)
    return gated @ w_out

def apply_rope(x, cos, sin):
    x1, x2 = jnp.split(x, 2, axis=-1)
    return jnp.concatenate([x1 * cos - x2 * sin, x2 * cos + x1 * sin], axis=-1)

def mla_mixer(h, positions, w_dq_dkv, q_norm_g, kv_norm_g, w_uq, w_ukv, w_o):
    B_, S_, _ = h.shape
    lat = h @ w_dq_dkv
    c_q, c_kv, k_rope = jnp.split(lat, [MLA_Q_LORA, MLA_Q_LORA + MLA_KV_LORA], axis=-1)
    c_q = rmsnorm(c_q, q_norm_g)
    c_kv = rmsnorm(c_kv, kv_norm_g)
    q = (c_q @ w_uq).reshape(B_, S_, MLA_HEADS, MLA_NOPE + MLA_ROPE)
    q_nope, q_rope = jnp.split(q, [MLA_NOPE], axis=-1)
    kv = (c_kv @ w_ukv).reshape(B_, S_, MLA_HEADS, MLA_NOPE + MLA_V)
    k_nope, v = jnp.split(kv, [MLA_NOPE], axis=-1)
    inv_freq = ROPE_THETA ** (-jnp.arange(0, MLA_ROPE, 2, dtype=jnp.float32) / MLA_ROPE)
    ang = positions.astype(jnp.float32)[..., None] * inv_freq
    cos, sin = jnp.cos(ang), jnp.sin(ang)
    q_rope = apply_rope(q_rope.astype(jnp.float32), cos[:, :, None], sin[:, :, None]).astype(h.dtype)
    k_rope = apply_rope(k_rope.astype(jnp.float32), cos, sin).astype(h.dtype)
    sm_scale = (MLA_NOPE + MLA_ROPE) ** -0.5
    nb = S_ // Q_BLOCK

    def to_blocks(t):
        return jnp.moveaxis(t.reshape(B_, nb, Q_BLOCK, *t.shape[2:]), 1, 0)

    k_idx = jnp.arange(S_)

    def attend_block(args):
        qn, qr, blk = args
        s = jnp.einsum('bqhd,bkhd->bhqk', qn, k_nope, preferred_element_type=jnp.float32)
        s = s + jnp.einsum('bqhr,bkr->bhqk', qr, k_rope, preferred_element_type=jnp.float32)
        q_idx = blk * Q_BLOCK + jnp.arange(Q_BLOCK)
        causal = k_idx[None, :] <= q_idx[:, None]
        s = jnp.where(causal[None, None], s * sm_scale, -1e30)
        p = jax.nn.softmax(s, axis=-1).astype(v.dtype)
        return jnp.einsum('bhqk,bkhd->bqhd', p, v)

    out = lax.map(attend_block, (to_blocks(q_nope), to_blocks(q_rope), jnp.arange(nb)))
    out = jnp.moveaxis(out, 0, 1).reshape(B_, S_, MLA_HEADS * MLA_V)
    return out @ w_o

def sq_relu_mlp(h, w1, w2):
    return jnp.square(jax.nn.relu(h @ w1)) @ w2

def first_inputs(seed: int = 0) -> dict:
    key = jax.random.key(seed)
    ks = jax.random.split(key, 32)
    f32 = jnp.float32

    def nrm(k, shape, std):
        return jax.random.normal(k, shape, f32) * std

    def gain(k, shape):
        return 1.0 + 0.1 * jax.random.normal(k, shape, f32)

    x = jax.random.normal(ks[0], (BATCH, SEQ, D_MODEL), f32)
    c = jax.random.normal(ks[1], (BATCH, D_MODEL), f32)
    offset = jax.random.randint(ks[2], (BATCH, 1), 0, MAX_POS_OFFSET, dtype=jnp.int32)
    positions = (offset + jnp.arange(SEQ, dtype=jnp.int32)[None, :]).astype(jnp.int32)
    return {
        'x': x,
        'c': c,
        'positions': positions,
        'ada_w': nrm(ks[3], (DEPTH, D_MODEL, 6 * D_MODEL), 0.5 * D_MODEL ** -0.5),
        'ada_b': nrm(ks[4], (DEPTH, 6 * D_MODEL), 0.02),
        'norm_mix_g': gain(ks[5], (DEPTH, D_MODEL)),
        'norm_mlp_g': gain(ks[6], (DEPTH, D_MODEL)),
        'pool_w': nrm(ks[7], (N_POOL_LAYERS, POOL_GROUPS, POOL_GROUP_DIM, POOL_GROUP_DIM), POOL_GROUP_DIM ** -0.5),
        'pool_scale': gain(ks[8], (N_POOL_LAYERS, D_MODEL)),
        'sgu_w_in': nrm(ks[9], (N_SGU_LAYERS, D_MODEL, 2 * SGU_WIDTH), D_MODEL ** -0.5),
        'sgu_ln_g': gain(ks[10], (N_SGU_LAYERS, SGU_WIDTH)),
        'sgu_ln_b': nrm(ks[11], (N_SGU_LAYERS, SGU_WIDTH), 0.02),
        'sgu_w_s': nrm(ks[12], (N_SGU_LAYERS, SGU_HEADS, SGU_CHUNK, SGU_CHUNK), SGU_CHUNK ** -0.5),
        'sgu_b_s': gain(ks[13], (N_SGU_LAYERS, SGU_HEADS, SGU_CHUNK)),
        'sgu_w_out': nrm(ks[14], (N_SGU_LAYERS, SGU_WIDTH, D_MODEL), SGU_WIDTH ** -0.5),
        'mla_w_dq_dkv': nrm(ks[15], (N_MLA_LAYERS, D_MODEL, MLA_Q_LORA + MLA_KV_LORA + MLA_ROPE), D_MODEL ** -0.5),
        'mla_q_norm_g': gain(ks[16], (N_MLA_LAYERS, MLA_Q_LORA)),
        'mla_kv_norm_g': gain(ks[17], (N_MLA_LAYERS, MLA_KV_LORA)),
        'mla_w_uq': nrm(ks[18], (N_MLA_LAYERS, MLA_Q_LORA, MLA_HEADS * (MLA_NOPE + MLA_ROPE)), MLA_Q_LORA ** -0.5),
        'mla_w_ukv': nrm(ks[19], (N_MLA_LAYERS, MLA_KV_LORA, MLA_HEADS * (MLA_NOPE + MLA_V)), MLA_KV_LORA ** -0.5),
        'mla_w_o': nrm(ks[20], (N_MLA_LAYERS, MLA_HEADS * MLA_V, D_MODEL), (MLA_HEADS * MLA_V) ** -0.5),
        'mlp_w1': nrm(ks[21], (DEPTH, D_MODEL, D_FF), D_MODEL ** -0.5),
        'mlp_w2': nrm(ks[22], (DEPTH, D_FF, D_MODEL), D_FF ** -0.5),
        'final_g': gain(ks[23], (D_MODEL,)),
    }

def first_block(x, c, positions, ada_w, ada_b, norm_mix_g, norm_mlp_g, pool_w, pool_scale,
              sgu_w_in, sgu_ln_g, sgu_ln_b, sgu_w_s, sgu_b_s, sgu_w_out,
              mla_w_dq_dkv, mla_q_norm_g, mla_kv_norm_g, mla_w_uq, mla_w_ukv, mla_w_o,
              mlp_w1, mlp_w2, final_g):
    c_act = jax.nn.silu(c)
    for i in range(DEPTH):
        mod = c_act @ ada_w[i] + ada_b[i]
        sh1, sc1, g1, sh2, sc2, g2 = jnp.split(mod, 6, axis=-1)
        h = modulate(rmsnorm(x, norm_mix_g[i]), sh1, sc1)
        kind, j = i % N_MIXERS, i // N_MIXERS
        if kind == 0:
            y = pool_mixer(h, pool_w[j], pool_scale[j])
        elif kind == 1:
            y = sgu_mixer(h, sgu_w_in[j], sgu_ln_g[j], sgu_ln_b[j], sgu_w_s[j], sgu_b_s[j], sgu_w_out[j])
        else:
            y = mla_mixer(h, positions, mla_w_dq_dkv[j], mla_q_norm_g[j], mla_kv_norm_g[j],
                          mla_w_uq[j], mla_w_ukv[j], mla_w_o[j])
        x = x + g1[:, None, :] * y
        h = modulate(rmsnorm(x, norm_mlp_g[i]), sh2, sc2)
        x = x + g2[:, None, :] * sq_relu_mlp(h, mlp_w1[i], mlp_w2[i])
    return rmsnorm(x, final_g)


DEPTH_2 = 1

GRID_W = 64
HEAD_DIM = 64
D_MIX = D_MODEL
A_HEADS = 8
A_KV_HEADS = 2
B_HEADS = 8
A_WIDTH = A_HEADS * HEAD_DIM
A_KV_WIDTH = A_KV_HEADS * HEAD_DIM
B_WIDTH = B_HEADS * HEAD_DIM
SPLITS = (A_WIDTH, A_KV_WIDTH, A_KV_WIDTH, A_WIDTH, B_WIDTH, B_WIDTH, B_WIDTH, B_WIDTH)
D_IN = sum(SPLITS)
AXIS_DIM = HEAD_DIM // 2
ROPE_PAIRS = AXIS_DIM // 2
NA_KH = 8
NA_KW = 16
NA_COL_BLOCK = 16
NA_BAND = NA_COL_BLOCK + NA_KW
EPS = 1e-6


def _rmsnorm(x, gain):
    x32 = x.astype(jnp.float32)
    y = x32 * lax.rsqrt(jnp.mean(x32 * x32, axis=-1, keepdims=True) + EPS)
    return (y * gain.astype(jnp.float32)).astype(x.dtype)

def _axial_rope_tables(seq, dtype):
    t = jnp.arange(seq, dtype=jnp.int32)
    row = (t // GRID_W).astype(jnp.float32)
    col = (t % GRID_W).astype(jnp.float32)
    inv = ROPE_THETA ** (-jnp.arange(ROPE_PAIRS, dtype=jnp.float32) * (2.0 / AXIS_DIM))
    ang_r = row[:, None] * inv[None, :]
    ang_c = col[:, None] * inv[None, :]
    ang = jnp.concatenate([ang_r, ang_r, ang_c, ang_c], axis=-1)
    return jnp.cos(ang)[:, None, :].astype(dtype), jnp.sin(ang)[:, None, :].astype(dtype)

def _rotate_half_axial(x):
    shp = x.shape
    xr = x.reshape(shp[:-1] + (2, 2, ROPE_PAIRS))
    x1 = xr[..., 0, :]
    x2 = xr[..., 1, :]
    return jnp.stack([-x2, x1], axis=-2).reshape(shp)

def _gqa_blocked(q, k, v):
    b, s, h, d = q.shape
    hk = k.shape[2]
    g = h // hk
    nb = s // Q_BLOCK
    qb = q.reshape(b, nb, Q_BLOCK, hk, g, d).transpose(1, 0, 2, 3, 4, 5)
    scale = d ** -0.5

    def block(qi):
        sc = jnp.einsum('bqkgd,bskd->bkgqs', qi, k).astype(jnp.float32) * scale
        p = jax.nn.softmax(sc, axis=-1).astype(v.dtype)
        return jnp.einsum('bkgqs,bskd->bqkgd', p, v)

    o = lax.map(block, qb)
    return o.transpose(1, 0, 2, 3, 4, 5).reshape(b, s, h * d)

def _neighbourhood_attn(q, k, v, rpb):
    b, s, h, d = q.shape
    rows = s // GRID_W
    kh = min(NA_KH, rows)
    n_cb = GRID_W // NA_COL_BLOCK
    qg = q.reshape(b, rows, GRID_W, h, d)
    kg = k.reshape(b, rows, GRID_W, h, d)
    vg = v.reshape(b, rows, GRID_W, h, d)
    c = np.arange(GRID_W)
    col_start = np.clip(c - NA_KW // 2, 0, GRID_W - NA_KW)
    band_start = np.clip(np.arange(n_cb) * NA_COL_BLOCK - NA_KW // 2, 0, GRID_W - NA_BAND)
    band_cols = band_start[:, None] + np.arange(NA_BAND)[None, :]
    qc = c.reshape(n_cb, NA_COL_BLOCK)
    qcs = col_start.reshape(n_cb, NA_COL_BLOCK)
    kc = band_cols[:, None, :]
    col_valid = (kc >= qcs[..., None]) & (kc < qcs[..., None] + NA_KW)
    col_idx = np.clip(kc - qc[..., None] + (NA_KW - 1), 0, 2 * NA_KW - 2)
    rpb_col = rpb[:, :, col_idx]
    mask = jnp.asarray(col_valid[:, :, None, :])
    scale = d ** -0.5

    def row_block(args):
        r, q_row = args
        r0 = jnp.clip(r - kh // 2, 0, rows - kh)
        k_rows = lax.dynamic_slice_in_dim(kg, r0, kh, axis=1)
        v_rows = lax.dynamic_slice_in_dim(vg, r0, kh, axis=1)
        k_band = jnp.take(k_rows, band_cols, axis=2)
        v_band = jnp.take(v_rows, band_cols, axis=2)
        qb = q_row.reshape(b, n_cb, NA_COL_BLOCK, h, d)
        sc = jnp.einsum('bjqhd,bkjchd->bhjqkc', qb, k_band).astype(jnp.float32) * scale
        row_idx = r0 + jnp.arange(kh) - r + (NA_KH - 1)
        bias = rpb_col[:, row_idx].transpose(0, 2, 3, 1, 4)
        sc = jnp.where(mask, sc + bias.astype(jnp.float32), -jnp.inf)
        p = jax.nn.softmax(sc, axis=(-2, -1)).astype(v.dtype)
        o = jnp.einsum('bhjqkc,bkjchd->bjqhd', p, v_band)
        return o.reshape(b, GRID_W, h * d)

    o = lax.map(row_block, (jnp.arange(rows), qg.transpose(1, 0, 2, 3, 4)))
    return o.transpose(1, 0, 2, 3).reshape(b, s, h * d)

def second_inputs(seed: int = 0) -> dict:
    key = jax.random.key(seed)
    ks = jax.random.split(key, 9)
    x = jax.random.normal(ks[0], (BATCH, SEQ, D_MODEL), jnp.float32)
    norm_gain = 1.0 + 0.02 * jax.random.normal(ks[1], (DEPTH_2, D_MODEL), jnp.float32)
    w_in = jax.random.normal(ks[2], (DEPTH_2, D_MODEL, D_IN), jnp.float32) * D_MODEL ** -0.5
    q_norm_a = 1.0 + 0.02 * jax.random.normal(ks[3], (DEPTH_2, HEAD_DIM), jnp.float32)
    k_norm_a = 1.0 + 0.02 * jax.random.normal(ks[4], (DEPTH_2, HEAD_DIM), jnp.float32)
    na_rpb = 0.02 * jax.random.normal(ks[5], (DEPTH_2, B_HEADS, 2 * NA_KH - 1, 2 * NA_KW - 1), jnp.float32)
    w_out = jax.random.normal(ks[6], (DEPTH_2, D_MIX, D_MODEL), jnp.float32) * D_MIX ** -0.5
    final_norm_gain = 1.0 + 0.02 * jax.random.normal(ks[7], (D_MODEL,), jnp.float32)
    return {"x": x, "norm_gain": norm_gain, "w_in": w_in, "q_norm_a": q_norm_a,
            "k_norm_a": k_norm_a, "na_rpb": na_rpb, "w_out": w_out,
            "final_norm_gain": final_norm_gain}

def second_block(x, norm_gain, w_in, q_norm_a, k_norm_a, na_rpb, w_out, final_norm_gain):
    b, s, _ = x.shape
    cos, sin = _axial_rope_tables(s, x.dtype)
    split_at = [int(v) for v in np.cumsum(SPLITS)[:-1]]
    for l in range(DEPTH_2):
        h = _rmsnorm(x, norm_gain[l])
        proj = h @ w_in[l]
        q_a, k_a, v_a, g_a, q_b, k_b, v_b, g_b = jnp.split(proj, split_at, axis=-1)
        q_a = _rmsnorm(q_a.reshape(b, s, A_HEADS, HEAD_DIM), q_norm_a[l])
        k_a = _rmsnorm(k_a.reshape(b, s, A_KV_HEADS, HEAD_DIM), k_norm_a[l])
        q_a = q_a * cos + _rotate_half_axial(q_a) * sin
        k_a = k_a * cos + _rotate_half_axial(k_a) * sin
        v_a = v_a.reshape(b, s, A_KV_HEADS, HEAD_DIM)
        o_a = _gqa_blocked(q_a, k_a, v_a) * jax.nn.silu(g_a)
        o_b = _neighbourhood_attn(q_b.reshape(b, s, B_HEADS, HEAD_DIM),
                                  k_b.reshape(b, s, B_HEADS, HEAD_DIM),
                                  v_b.reshape(b, s, B_HEADS, HEAD_DIM), na_rpb[l])
        o_b = o_b * jax.nn.silu(g_b)
        mixed = jnp.concatenate([o_a, o_b], axis=-1)
        x = x + mixed @ w_out[l]
    return _rmsnorm(x, final_norm_gain)


def setup_inputs(seed=0):
    out = dict(first_inputs(seed))
    for name, value in second_inputs(seed + 1).items():
        if name != "x":
            out[name + "_2"] = value
    return out


def reference(
    x, c, positions, ada_w, ada_b, norm_mix_g, norm_mlp_g, pool_w, pool_scale, sgu_w_in,
    sgu_ln_g, sgu_ln_b, sgu_w_s, sgu_b_s, sgu_w_out, mla_w_dq_dkv, mla_q_norm_g, mla_kv_norm_g,
    mla_w_uq, mla_w_ukv, mla_w_o, mlp_w1, mlp_w2, final_g, norm_gain_2, w_in_2, q_norm_a_2,
    k_norm_a_2, na_rpb_2, w_out_2, final_norm_gain_2,
):
    x = first_block(
        x, c, positions, ada_w, ada_b, norm_mix_g, norm_mlp_g, pool_w, pool_scale, sgu_w_in,
        sgu_ln_g, sgu_ln_b, sgu_w_s, sgu_b_s, sgu_w_out, mla_w_dq_dkv, mla_q_norm_g,
        mla_kv_norm_g, mla_w_uq, mla_w_ukv, mla_w_o, mlp_w1, mlp_w2, final_g,
    )
    return second_block(
        x, norm_gain_2, w_in_2, q_norm_a_2, k_norm_a_2, na_rpb_2, w_out_2, final_norm_gain_2,
    )


_drawn_inputs = setup_inputs


def setup_inputs(seed=0):
    import zlib

    import numpy as np

    out = dict(_drawn_inputs(seed))
    spreads = {}
    factors = {'sgu_ln_g': 4.222,
     'sgu_ln_b': 8.0,
     'sgu_b_s': 2.808,
     'norm_gain_2': 8.0,
     'q_norm_a_2': 8.0,
     'k_norm_a_2': 8.0,
     'na_rpb_2': 35.89,
     'final_norm_gain_2': 7.776}
    for name, (base, spread) in spreads.items():
        noise = np.random.default_rng([zlib.crc32(name.encode()), seed]).standard_normal(out[name].shape)
        drawn = base * np.exp(spread * noise) if base else spread * noise
        out[name] = __import__('jax').numpy.asarray(drawn.astype(out[name].dtype))
    for name, factor in factors.items():
        out[name] = (out[name] * factor).astype(out[name].dtype)
    return out
```

```python
import concourse.bass as bass
import numpy as np
from concourse import mybir

F32 = mybir.dt.float32
F32R = mybir.dt.float32r
ALU = mybir.AluOpType
ACT = mybir.ActivationFunctionType
AX_X = mybir.AxisListType.X

P = 128
S = 1024
D = 1024
KT = D // P
NH = 2
H = S // NH
F = 4 * D
UC = 256
UNIT = KT * UC
CHUNKS = F // UC
FT = UC // P
MODS = 6 * KT
STAGES = 4
A_BANKS, D_BANKS = 2, 4
WINDOWS = (2, 4, 8, 16)
HD = 64
QT = S // P
GRID = 64
ROWS = S // GRID
NKH, NKW = 8, 16
SLOTS = 8
PAIR = 2 * QT
EPS = 1e-6
LN_EPS = 1e-5

COLS = {}
_at = 0
for _name, _n in (("c", KT), ("ada_b0", MODS), ("ada_b1", MODS), ("mix_g0", KT), ("mix_g1", KT),
                  ("mlp_g0", KT), ("mlp_g1", KT), ("pool_scale", KT), ("ln_g", KT), ("ln_b", KT),
                  ("final_g", KT), ("gain2", KT), ("final2", KT), ("qg", 1), ("kg", 1)):
    COLS[_name] = (_at, _at + _n)
    _at += _n
NCOLS = _at

def neighbourhood(qt):
    first = [min(max(r - NKH // 2, 0), ROWS - NKH) for r in (2 * qt, 2 * qt + 1)]
    return first[0], first[1] + NKH - first[0]


CONST = {}
_at = 0
for _name, _n in (("ident", P), ("tri", P), ("pairs", P), ("rot", P), ("invc", 4 * 16)):
    CONST[_name] = (_at, _at + _n)
    _at += _n
NCONST = _at


class Tally:

    def __init__(self):
        self.n = dict.fromkeys("u w c uc un a d t h b q s n sp ada mod x g o ol r v v2 vg".split(), 0)
        self.reg, self.per = None, {}
        self.stored = [0] * SLOTS

    def __call__(self, name, more=0):
        v = self.n[name] + more
        return self.reg * self.per[name] + v if self.reg is not None and self.per.get(name) else v

    def add(self, **more):
        for name, k in more.items():
            self.n[name] += k

    def b_units(self, u):
        return self("v", u - 4 * PAIR)

    def masked(self, e):
        v = (self.n["v"] // PAIR - 4) * 2 + e + 1
        return self.reg * 2 + v if self.reg is not None else v

    def loads(self, n, first=0):
        v = (self.n["v"] // PAIR + 1 - first) * n
        return self.reg * (self.per["v"] // PAIR * n) + v if self.reg is not None else v

    def fill(self):
        v = self.n["u"] // STAGES + 1
        return self.reg * (self.per["u"] // STAGES) + v if self.reg is not None else v

    def loop(self, eng, count, per, body):
        start = dict(self.n)
        with eng.Fori(0, count) as i:
            self.reg, self.per = i, per
            body(i)
            self.reg = None
        for name in self.n:
            assert name == "uc" or self.n[name] == start[name] + per.get(name, 0), name
            self.n[name] = start[name] + count * per.get(name, 0)


def reach(eng, sem, count):
    if not isinstance(count, int) or count > 0:
        eng.wait_ge(sem, count)



def build(nc, x_in, cols_in, const_in, ada_w, pool_w, sgu_in, sgu_ws, sgu_bs, sgu_out, w1, w2,
          rope_in, mask_in, w_in2, rpb, w_out2, out):
    top = [(nc.sbuf_base + 31) // 32 * 32]

    def sb(name, shape, dt=F32, at=None):
        size = 4 * int(np.prod(shape[1:]))
        where = top[0] if at is None else at
        if at is None:
            top[0] += (size + 31) // 32 * 32
        assert where + size <= nc.sbuf_usable_end, name
        return nc.alloc_sbuf_tensor_at(name, shape, dt, offset=where)

    cols = sb("cols", [P, NCOLS])
    const = sb("const", [P, NCONST])
    ones = sb("ones", [P, P])
    epsc = sb("epsc", [P, 2])
    c_act = sb("c_act", [P, KT])
    mod = sb("mod", [P, 2, MODS])
    gain = sb("gain", [P, 4, KT])
    pg = sb("pg", [P, KT])
    std = sb("std", [P, 4])
    rstd = sb("rstd", [P, 4])
    x_at = top[0]
    X = sb("X", [P, KT, S])
    h_at = top[0]
    Hhi = sb("Hhi", [P, KT, S], F32R)
    Hlo = sb("Hlo", [P, KT, S], F32R)
    m_at = top[0]
    Mhi = sb("Mhi", [P, 2, FT, S], F32R)
    Mlo = sb("Mlo", [P, 2, FT, S], F32R)
    Whi = sb("Whi", [P, 2, UNIT], F32R)
    Wlo = sb("Wlo", [P, 2, UNIT], F32R)
    stage = sb("stage", [P, STAGES, UNIT])
    t_at = top[0]
    TA = sb("TA", [P, 2, H])
    TB = sb("TB", [P, 2, H])
    SQ = sb("SQ", [P, 2, H])
    SUM = sb("SUM", [P, H])
    diag = sb("diag", [P, H])
    acc_at = top[0]
    acc = sb("acc", [P, D])
    Vhi = sb("Vhi", [P, 2, KT, P], F32R, at=t_at)
    Vlo = sb("Vlo", [P, 2, KT, P], F32R, at=t_at + 4 * 2 * S)
    ws = sb("ws", [P, KT, P], at=acc_at)
    bs = sb("bs", [P, KT, P])
    WShi = sb("WShi", [P, 2, P], F32R)
    WSlo = sb("WSlo", [P, 2, P], F32R)
    V = sb("V", [P, KT, D], at=m_at)
    bstat = sb("bstat", [P, KT, 2, 6], at=t_at)
    mv = sb("mv", [P, KT, 2])
    vstd = sb("vstd", [P, KT])
    vrs = sb("vrs", [P, KT])
    PAD = 16
    PH = sb("PH", [P, 2, PAD + S], at=m_at)
    PS = sb("PS", [P, 2, PAD + S], at=m_at + 8 * (PAD + S))
    PO = sb("PO", [P, 2, S], at=m_at + 16 * (PAD + S))
    PF = sb("PF", [P, 16], at=m_at + 24 * (PAD + S))

    QX = nc.dram_tensor("q_heads", (2, 16, HD, S), F32).ap()
    KX = nc.dram_tensor("k_heads", (2, 12, HD, S), F32).ap()
    VX = nc.dram_tensor("v_heads", (12, S, 2, HD), F32).ap()
    SG = nc.dram_tensor("silu_gates", (D, S), F32).ap()
    NF, NI = 14 * GRID, 9 * GRID
    BX = nc.dram_tensor("position_bias", (8, P, NF + NI), F32).ap()
    OH = sb("OH", [P, SLOTS, H], F32R, at=m_at)
    OL = sb("OL", [P, SLOTS, H], F32R, at=m_at + 4 * SLOTS * H)
    OF = sb("OF", [P, SLOTS, H], at=m_at)
    rope = sb("rope", [P, 2, S], at=x_at)
    QN = sb("QN", [P, 2, H], at=x_at + 8 * S)
    RT = sb("RT", [P, 2, H], at=x_at + 12 * S)
    RF = sb("RF", [P, 2, H], at=x_at + 16 * S)
    qg8 = sb("qg8", [P, 2])
    QS = sb("QS", [P, 2, S], F32R, at=m_at)
    KH = sb("KH", [P, 2, S], F32R, at=m_at + 8 * S)
    KL = sb("KL", [P, 2, S], F32R, at=m_at + 16 * S)
    VT = sb("VT", [P, 2, QT, P], F32R, at=m_at + 24 * S)
    bias = sb("bias", [P, 2, NF + NI], at=m_at + 32 * S)
    mask = sb("mask", [P, NF + NI], at=m_at + 32 * S + 8 * (NF + NI))
    PE_ = sb("probs", [P, 2, S], at=t_at)
    DG = sb("inverse_sums", [P, 2, P], at=t_at + 8 * S)
    neg_max = sb("neg_max", [P, 4])
    den = sb("den", [P, 4])
    rden = sb("rden", [P, 4])
    PTh = sb("PTh", [P, 2, QT, H], F32R, at=h_at)
    PTl = sb("PTl", [P, 2, QT, H], F32R, at=h_at + 4 * KT * S)
    OT = sb("OT", [P, 2, H], at=acc_at)
    OS = sb("OS", [P, 2, H], at=acc_at + 8 * H)

    x_saved = nc.dram_tensor("x_saved", (D, S), F32).ap()

    PS_ALL = nc.alloc_psum_tensor("banks", [P, 8, H], F32)
    A, Dn, B6, B7 = PS_ALL[:, 0:2, :], PS_ALL[:, 2:6, :], PS_ALL[:, 6, :], PS_ALL[:, 7, :]
    SB_, TP, OB = PS_ALL[:, 0:4, :], PS_ALL[:, 4:6, :], PS_ALL[:, 6:8, :]

    def col(name):
        a, b = COLS[name]
        return cols[:, a:b]

    def con(name):
        a, b = CONST[name]
        return const[:, a:b]

    def half(hf):
        return slice(hf * H, (hf + 1) * H)

    sem = nc.alloc_semaphore
    cols_loaded, const_loaded, x_loaded = sem("cols_loaded"), sem("const_loaded"), sem("x_loaded")
    stage_in = [sem(f"stage_filled{i}") for i in range(STAGES)]
    unit_done = sem("unit_done")
    w_hi = sem("weight_hi")
    a_ready, a_free = sem("a_ready"), sem("a_free")
    d_ready, d_free = sem("d_ready"), sem("d_free")
    tb_ready = sem("tb_ready")
    ta_ready = sem("ta_ready")
    hi_done, lo_done = sem("hi_done"), sem("lo_done")
    sq_done, sum_done = sem("square_done"), sem("sum_done")
    stat_ready, std_ready = sem("stat_ready"), sem("std_ready")
    rstd_own, diag_ready, rstd_ready = sem("rstd_own"), sem("diag_ready"), sem("rstd_ready")
    ada_half, ada_sum, mod_done = sem("ada_half"), sem("ada_sum"), sem("mod_done")
    dve_own, c_ready, set_ready = sem("dve_own"), sem("c_ready"), sem("set_ready")
    gain_ready = sem("gain_ready")
    ws_loaded, ws_masked, bs_ready = sem("ws_loaded"), sem("ws_masked"), sem("bs_ready")
    x_stored, x_back = sem("x_stored"), sem("x_back")
    bs_own, row_sum = sem("bs_own"), sem("row_sum")
    v_std, v_norm = sem("v_std"), sem("v_norm")
    mixed_own = sem("mixed_own")
    x_scaled = sem("x_scaled")
    slot_stored = [sem(f"slot_stored{i}") for i in range(SLOTS)]
    out_hi, out_lo = sem("slot_hi"), sem("slot_lo")
    rope_loaded, bias_built = sem("rope_loaded"), sem("bias_built")
    head_copied, ss_ready, sd_done = sem("head_copied"), sem("head_sums"), sem("head_std")
    qn_done, rot_ready, rf_done = sem("head_normed"), sem("head_rotated"), sem("roped")
    qk_loaded = [sem(f"qk_loaded{i}") for i in range(2)]
    v_loaded = [sem(f"v_loaded{i}") for i in range(2)]
    bias_loaded = [sem(f"bias_loaded{i}") for i in range(2)]
    bias_masked, mask_loaded, gates_loaded = sem("bias_masked"), sem("mask_loaded"), sem("gates_loaded")
    s_ready, max_own, max_done, exp_done = sem("s_ready"), sem("max_own"), sem("max_done"), sem("exp_done")
    rd_own, rd_done = sem("rd_own"), sem("rd_done")
    t_ready, th_done, tl_done = sem("t_ready"), sem("th_done"), sem("tl_done")
    o_ready, ot_done, os_done, mixed_done = sem("o_ready"), sem("ot_done"), sem("os_done"), sem("mixed_done")
    po_ready, out_done = sem("pooled_ready"), sem("out_done")

    def src_in(w, c):
        return w.rearrange("(k p) n -> p k n", p=P)[:, :, bass.ds(c * UC, UC)]

    def src_w2(l, c):
        return w2[l].rearrange("(q p) n -> p q n", p=P)[:, bass.ds(c * FT, FT), :]

    def src_ada(l, cc, q):
        return ada_w[l].rearrange("(k p) n -> p k n", p=P)[:, 2 * q:2 * q + 2, bass.ds(cc * D, D)]

    src_pool = pool_w.rearrange("g (k p) n -> p (g k) n", p=P)

    def lagged(u, lag, kind, before):
        w = u - lag
        if w >= 0:
            return [(w, kind)]
        return [(w, before)] if before else []

    def banks(n):
        tiles = (n + P - 1) // P
        return [(0, 0, tiles // 2), (1, tiles // 2, tiles - tiles // 2)]

    def probs_t(x, u, k, m):
        return x[:, (u // 4) % 2, k:k + m, (u % 4) * P:(u % 4 + 1) * P]

    def width(kind, u):
        return S if kind == "A" else neighbourhood(u % QT)[1] * GRID

    def walk(eng, do):
        T = Tally()

        def ada(l, cc, q):
            do["ada"](T, l, cc, q)
            T.add(u=1, ada=1)

        def mods(l, cc):
            do["mods"](T, l, cc)
            T.add(mod=1)

        def split(src):
            do["split"](T, src)
            T.add(u=1, w=1)
            T.n["uc"], T.n["un"] = T.n["un"], T.n["u"]

        def stores(kind, *args):
            n, dmas = {"heads": lambda what, j, nf: (2 * nf, 2 if what == "q" else 8), "plain": lambda *_: (4, 2),
                       "vals": lambda head, at, n: (QT, 4 if n == P else 2), "silu": lambda j: (4, 1)}[kind](*args)
            for i in range(n):
                T.stored[(T.n["o"] + i) % SLOTS] += dmas

        def step(kind, nxt, counts, *args):
            if nxt is not None:
                split(nxt)
            else:
                T.n["uc"] = T.n["un"]
            do[kind](T, *args)
            if "o" in counts:
                stores(kind, *args)
            T.add(c=1, **counts)

        def norm(which):
            do["norm"](T, which)
            T.add(q=2 * KT, s=14, n=2, t=16, b=16, h=16, g=which < 4)

        A4 = dict(a=4, t=4, h=4)
        D16 = dict(d=16)

        do["start"](T)
        for cc in range(2):
            for q in range(4):
                ada(0, cc, q)
            mods(0, cc)
        split(src_pool)
        do["norm_pool"](T)
        T.add(q=2 * KT, s=14, n=2, t=16, b=16, h=KT, g=1)
        for cc in range(2, 6):
            for q in range(4):
                ada(0, cc, q)
            mods(0, cc)
        step("pool", src_in(w1[0], 0), D16)

        def mlp(l, ada_passes):
            def up(par, nxt, first=False):
                step("up", nxt, A4, par, first)

            def down(par, nxt, ahead=4):
                step("down", nxt, D16, mod[:, l, 5 * KT:6 * KT], par, ahead)

            def passes(first, count, with_ada):
                def body(i):
                    for half_pass in range(2):
                        c = 2 * (i + first) + half_pass
                        if with_ada:
                            ada(1, i, 2 * half_pass)
                        up(1 - half_pass, src_w2(l, c))
                        if with_ada:
                            ada(1, i, 2 * half_pass + 1)
                        down(half_pass, src_in(w1[l], c + 2))
                    if with_ada:
                        mods(1, i)

                per = dict(u=4, uc=4, un=4, w=4, c=4, a=8, d=32, t=8, h=8)
                if with_ada:
                    per.update(u=8, uc=8, un=8, ada=4, mod=1)
                T.loop(eng, count, per, body)

            up(0, src_in(w1[l], 1), first=True)
            if ada_passes:
                passes(0, ada_passes, True)
            passes(ada_passes, CHUNKS // 2 - 1 - ada_passes, False)
            up(1, src_w2(l, CHUNKS - 2))
            down(0, src_w2(l, CHUNKS - 1))

        norm(1)
        mlp(0, 6)
        step("down", src_in(sgu_in, 4), D16, mod[:, 0, 5 * KT:6 * KT], 1, 0)

        norm(2)
        do["spill"](T)
        T.add(sp=1)
        for j in range(4):
            step("values", src_in(sgu_in, (j + 5) % 8), dict(a=8), j)
        for j in range(4):
            step("gates", src_in(sgu_in, j + 1) if j < 3 else src_in(sgu_out, 0), dict(a=4), j)
            do["between"](T, j)
            if j >= 1:
                do["mix"](T, j - 1)
                T.add(d=4, h=4)
        do["mix"](T, 3)
        T.add(d=4, h=4)
        do["resplit"](T)
        T.add(h=KT)
        for j in range(4):
            step("project", src_in(sgu_out, j + 1) if j < 3 else src_in(w1[1], 0), dict(d=4),
                 j, mod[:, 1, 2 * KT:3 * KT], j == 0)
        norm(3)
        mlp(1, 0)
        step("down", src_in(w_in2, 0), D16, mod[:, 1, 5 * KT:6 * KT], 1, 0)
        do["scale_x"](T, "final_g", "down")
        T.add(q=2 * KT, s=14, n=2, x=2 * KT)

        norm(4)
        do["spill"](T)
        T.add(sp=1)

        def nxt(j):
            return src_in(w_in2, j + 1)

        for j in range(2):
            step("heads", nxt(j), dict(a=4, o=4, ol=4, r=4), "q", j, FT)
        step("heads", nxt(2), dict(a=2, o=2, ol=2, r=2), "k", 0, 1)
        T.add(c=-1)
        do["vals"](T, 0, P, P)
        stores("vals", 0, P, P)
        T.add(c=1, d=8, o=8, ol=8)
        for j in (3, 4):
            step("silu", nxt(j), dict(a=4, o=4), j - 3)
        for j in (5, 6):
            step("plain", nxt(j), dict(d=4, o=4, ol=4), "q", 8 + 4 * (j - 5))
        for j in (7, 8):
            step("plain", nxt(j), dict(d=4, o=4, ol=4), "k", 4 + 4 * (j - 7))
        for j in (9, 10):
            step("vals", nxt(j), dict(d=8, o=8, ol=8), 4 + 4 * (j - 9), 0, UC)
        for j in (11, 12):
            step("silu", nxt(j) if j < 12 else None, dict(a=4, o=4), 2 + j - 11)

        do["attend_start"](T)
        for kind in "AB":
            def pair(i, first=False, kind=kind):
                do["attend"](T, kind, i, ("A" if kind == "B" else None) if first else kind)
                T.add(v=PAIR, v2=2 * PAIR, vg=4)

            pair(0, first=True)
            T.loop(eng, 3, dict(v=PAIR, v2=2 * PAIR, vg=4), lambda i: pair(i + 1))
        do["attend_end"](T)
        split(src_in(w_out2, 0))
        do["resplit"](T)
        T.add(h=KT)
        for j in range(4):
            step("project", src_in(w_out2, j + 1) if j < 3 else None, dict(d=4), j, ones[:, 0:KT], j == 0)
        do["scale_x"](T, "final2", "project")
        T.add(q=2 * KT, s=14, n=2, x=2 * KT)
        do["finish"](T)

    block = nc.Block()
    with block:
        @block.sync
        def _(sync):
            def load(T, src):
                s = T.n["u"] % STAGES
                reach(sync, unit_done, T("u", 1 - STAGES))
                sync.dma_start(stage[:, s, :].rearrange("p (a n) -> p a n", a=src.shape[1]),
                               src).then_inc(stage_in[s], 16)

            def start(T):
                sync.dma_start(cols[:], cols_in).then_inc(cols_loaded, 16)
                for k in range(KT):
                    sync.dma_start(X[:, k, :], x_in[k * P:(k + 1) * P, :]).then_inc(x_loaded, 16)
                sync.dma_start(const[:], const_in).then_inc(const_loaded, 16)

            def spill(T):
                sync.wait_ge(tb_ready, T("b"))
                if T("sp") == 1:
                    sync.wait_ge(x_back, 16 * KT)
                for k in range(KT):
                    sync.dma_start(x_saved[k * P:(k + 1) * P, :], X[:, k, :]).then_inc(x_stored, 16)
                if T("sp") == 0:
                    build_bias(T)
                    sync.wait_ge(unit_done, T("u"))
                    sync.wait_ge(mod_done, T("mod"))
                    sync.dma_start(ws[:], sgu_ws.rearrange("h s t -> s h t")).then_inc(ws_loaded, 16)
                    sync.dma_start(bs[:].rearrange("p h t -> p (h t)"),
                                   bass.AP(sgu_bs.tensor, 0, [[0, P], [1, KT * P]])).then_inc(ws_loaded, 16)

            def resplit(T):
                sync.wait_ge(x_stored, 16 * KT * T("sp"))
                for k in range(KT):
                    sync.wait_ge(lo_done, T("h", k + 1))
                    sync.dma_start(X[:, k, :], x_saved[k * P:(k + 1) * P, :]).then_inc(x_back, 16)

            def heads(T, what, j, nf):
                if T.n["r"] == 0:
                    sync.wait_ge(x_stored, 16 * KT * T("sp"))
                    sync.dma_start(rope[:], rope_in.rearrange("c p n -> p c n")).then_inc(rope_loaded, 16)

            def attend_start(T):
                for s in range(SLOTS):
                    sync.wait_ge(slot_stored[s], 16 * T.stored[s])
                sync.wait_ge(unit_done, T("u"))
                sync.wait_ge(a_ready, T("a"))
                sync.wait_ge(d_ready, T("d"))
                sync.wait_ge(bias_built, 16 * 32)
                for k in range(KT):
                    sync.dma_start(X[:, k, :], SG[k * P:(k + 1) * P, :]).then_inc(gates_loaded, 16)
                sync.dma_start(mask[:], mask_in).then_inc(mask_loaded, 16)

            def build_bias(T):
                for h in range(8):
                    for par in range(2):
                        for row, n, at in ((1 - par, 14, 0), (3 - par, 9, NF)):
                            src = bass.AP(rpb.tensor, (h * 15 + row) * 127 + 63, [[127, n], [-1, GRID], [1, GRID]])
                            dst = BX[h, par * GRID:(par + 1) * GRID, at:at + n * GRID].rearrange("c (r k) -> r c k", k=GRID)
                            sync.dma_start(dst, src).then_inc(bias_built, 16)

            def finish(T):
                sync.wait_ge(d_free, T("d"))
                reach(sync, x_scaled, T("x"))
                for k in range(KT):
                    sync.dma_start(out[k * P:(k + 1) * P, :], X[:, k, :]).then_inc(out_done, 16)
                sync.wait_ge(out_done, 16 * KT)

            def nothing(T, *_):
                pass

            walk(sync, dict(start=start, ada=lambda T, l, cc, q: load(T, src_ada(l, cc, q)), mods=nothing,
                            split=load, norm_pool=nothing, norm=nothing, pool=nothing, up=nothing, down=nothing,
                            spill=spill, values=nothing, gates=nothing, between=nothing, mix=nothing, resplit=resplit,
                            project=nothing, scale_x=nothing, finish=finish, heads=heads, vals=nothing, silu=nothing, plain=nothing, attend_start=attend_start, attend=nothing,
                            attend_end=nothing))

        @block.gpsimd
        def _(pool):
            def start(T):
                nc.gpsimd.memset(ones[:], 1.0).then_inc(set_ready, 1)
                nc.gpsimd.memset(epsc[:, 0:1], EPS).then_inc(set_ready, 1)
                nc.gpsimd.memset(epsc[:, 1:2], LN_EPS).then_inc(set_ready, 1)
                nc.gpsimd.memset(PH[:, :, 0:PAD], 0.0).then_inc(set_ready, 1)
                nc.gpsimd.memset(PS[:, :, 0:PAD], 0.0).then_inc(set_ready, 1)

            def norm(T, which=None):
                for hf in range(NH):
                    s, q = T.n["s"] + 7 * hf, T.n["q"] + KT * hf
                    reach(pool, stat_ready, T("n", hf))
                    for k in range(1, KT):
                        pool.wait_ge(sq_done, q + k + 1)
                        if k > 1:
                            pool.wait_ge(sum_done, s + k - 1)
                        first = SQ[:, 0, :] if k == 1 else SUM[:]
                        nc.gpsimd.tensor_tensor(SUM[:], first, SQ[:, k % 2, :], ALU.add).then_inc(sum_done, 1)

            def nothing(T, *_):
                pass

            def spill(T):
                if T("sp") == 0:
                    pool.wait_ge(ws_loaded, 32)
                    for h in range(KT):
                        nc.gpsimd.tensor_tensor(ws[:, h, :], ws[:, h, :], con("tri"), ALU.mult).then_inc(ws_masked, 1)

            def store(T, i, n_dma, lo, pairs):
                pool.wait_ge(out_hi, T("o", i + 1))
                if lo is not None:
                    pool.wait_ge(out_lo, T("ol", lo + 1))
                for dst, src in pairs:
                    nc.gpsimd.dma_start(dst, src).then_inc(slot_stored[(T.n["o"] + i) % SLOTS], 16)

            def out_slot(T, i):
                s = (T.n["o"] + i) % SLOTS
                return OH[:, s, :].bitcast(F32), OL[:, s, :].bitcast(F32), OF[:, s, :]

            def heads(T, what, j, nf):
                for i in range(2 * nf):
                    hf, f = i // nf, i % nf
                    hi, lo, _ = out_slot(T, i)
                    if what == "q":
                        pairs = [(QX[s, 4 * j + 2 * f:4 * j + 2 * f + 2, :, half(hf)].rearrange("h p n -> (h p) n"), t)
                                 for s, t in enumerate((hi, lo))]
                    else:
                        pairs = [(KX[s, 2 * kv + r, :, half(hf)], t[HD * kv:HD * kv + HD])
                                 for s, t in enumerate((hi, lo)) for kv in range(2) for r in range(2)]
                    store(T, i, len(pairs), i, pairs)

            def plain(T, what, head):
                dst = QX if what == "q" else KX
                for i in range(4):
                    hf, f = i // 2, i % 2
                    hi, lo, _ = out_slot(T, i)
                    store(T, i, 2, i, [(dst[s, head + 2 * f:head + 2 * f + 2, :, half(hf)].rearrange("h p n -> (h p) n"),
                                        t) for s, t in enumerate((hi, lo))])

            def vals(T, head, at, n):
                for i in range(QT):
                    hi, lo, _ = out_slot(T, i)
                    tok = slice(i * P, (i + 1) * P)
                    pairs = []
                    for s, t in enumerate((hi, lo)):
                        t = t[:, 0:n].rearrange("p (h d) -> p h d", d=HD)
                        if n == P:
                            for r in range(2):
                                pairs.append((VX[r:4:2, tok, s, :].rearrange("h p d -> p h d"), t))
                        else:
                            pairs.append((VX[head:head + 4, tok, s, :].rearrange("h p d -> p h d"), t))
                    store(T, i, len(pairs), i, pairs)

            def silu(T, j):
                for i in range(4):
                    hf, f = i // 2, i % 2
                    row = (j * FT + f) * P
                    store(T, i, 1, None, [(SG[row:row + P, half(hf)], out_slot(T, i)[2])])

            def load_heads(T, kind, i, e):
                if kind == "A":
                    head = 2 * i + e
                    kv = i
                else:
                    head = 2 * i + e + 8
                    kv = 2 * i + e + 4
                reach(pool, o_ready, T("vg", 2 * e - 2))
                if T.n["v"] == 0 and e == 0:
                    for s in range(SLOTS):
                        pool.wait_ge(slot_stored[s], 16 * T.stored[s])
                for s in range(2):
                    part = slice(s * HD, (s + 1) * HD)

                    def one(x, j):
                        return x[:, bass.ds(j, 1), :, :].rearrange("s h p n -> s (h p) n")

                    nc.gpsimd.dma_start(QS[part, e, :].bitcast(F32), one(QX, head)[s]).then_inc(qk_loaded[e], 16)
                    nc.gpsimd.dma_start(KH[part, e, :].bitcast(F32), one(KX, kv)[0]).then_inc(qk_loaded[e], 16)
                    nc.gpsimd.dma_start(KL[part, e, :].bitcast(F32), one(KX, kv)[1]).then_inc(qk_loaded[e], 16)
                for k in (0, QT // 2):
                    nc.gpsimd.dma_start(VT[:, e, k:k + QT // 2].bitcast(F32),
                                        VX[bass.ds(kv, 1), k * P:(k + QT // 2) * P]
                                        .rearrange("a (k p) s d -> p (a k) (s d)", p=P)).then_inc(v_loaded[e], 16)
                if kind == "B":
                    reach(pool, exp_done, T("v", QT * (e - 1)))
                    nc.gpsimd.dma_start(bias[:, e, :], BX[bass.ds(2 * i + e, 1)].rearrange("a p n -> p (a n)")) \
                        .then_inc(bias_loaded[e], 16)

            def mask_bias(T, e):
                pool.wait_ge(bias_loaded[e], T.loads(16, 4))
                pool.wait_ge(mask_loaded, 16)
                nc.gpsimd.tensor_tensor(bias[:, e, :], bias[:, e, :], mask[:], ALU.add).then_inc(bias_masked, 1)

            def attend(T, kind, i, before):
                for e in range(2):
                    load_heads(T, kind, i, e)
                    if kind == "B":
                        mask_bias(T, e)

            walk(pool, dict(start=start, ada=nothing, mods=nothing, split=nothing, norm_pool=norm, norm=norm,
                            pool=nothing, up=nothing, down=nothing, spill=spill, values=nothing, gates=nothing,
                            between=nothing, mix=nothing, resplit=nothing, project=nothing, scale_x=lambda T, *_: norm(T),
                            finish=nothing, heads=heads, vals=vals, silu=silu, plain=plain, attend_start=nothing, attend=attend,
                            attend_end=nothing))

        @block.scalar
        def _(act):
            def start(T):
                act.wait_ge(cols_loaded, 16)
                nc.scalar.activation(c_act[:], col("c"), ACT.Silu).then_inc(c_ready, 1)

            def split(T, src):
                s = T.n["u"] % STAGES
                act.wait_ge(stage_in[s], T.fill() * 16)
                reach(act, a_ready, T("a"))
                reach(act, d_ready, T("d"))
                nc.scalar.activation(Whi[:, T.n["w"] % 2, :], stage[:, s, :], ACT.Copy).then_inc(w_hi, 1)

            def squares(T, hf, source="down"):
                s = T.n["s"] + 7 * hf
                for k in range(KT):
                    if source == "dram":
                        act.wait_ge(x_loaded, 16 * KT)
                    elif source == "project":
                        act.wait_ge(d_free, T("d", 4 * (k // 2) + 2 * hf + k % 2 + 1 - 16))
                    elif source == "scaled":
                        act.wait_ge(x_scaled, T("x", KT * hf + k + 1 - 16))
                    else:
                        act.wait_ge(d_free, T("d", KT * hf + k + 1 - 16))
                    reach(act, sum_done, s + max(k - 1, 0))
                    nc.scalar.activation(SQ[:, k % 2, :], X[:, k, half(hf)], ACT.Square).then_inc(sq_done, 1)
                act.wait_ge(set_ready, 5)
                act.wait_ge(stat_ready, T("n", hf + 1))
                reach(act, rstd_own, T("n", hf))
                nc.scalar.activation(std[:], B6[:, 0:4], ACT.Sqrt, scale=1.0 / D,
                                     bias=epsc[:, 0:1]).then_inc(std_ready, 1)

            def norm_pool(T):
                for hf in range(NH):
                    squares(T, hf, "dram")
                act.wait_ge(gain_ready, T("g", 1))

                def pooled_hi(k):
                    act.wait_ge(po_ready, k + 1)
                    nc.scalar.activation(Hhi[:, k, :], PO[:, k % 2, :], ACT.Copy).then_inc(hi_done, 1)

                for k in range(KT):
                    if k >= 2:
                        act.wait_ge(po_ready, k - 1)
                    for hf in range(NH):
                        act.wait_ge(tb_ready, T("b", 2 * k + hf + 1))
                        nc.scalar.activation(PH[:, k % 2, PAD + hf * H:PAD + (hf + 1) * H], TB[:, hf, :],
                                             ACT.Identity, scale=gain[:, 0, k:k + 1],
                                             bias=mod[:, 0, k:k + 1]).then_inc(ta_ready, 1)
                    if k >= 1:
                        pooled_hi(k - 1)
                pooled_hi(KT - 1)

            def norm(T, which):
                if which == 4:
                    scale, shift = col("gain2"), None
                else:
                    scale, shift = gain[:, which, :], mod[:, which // 2, (which % 2) * 3 * KT:][:, 0:KT]
                for hf in range(NH):
                    squares(T, hf, {3: "project", 4: "scaled"}.get(which, "down"))
                    if which < 4 and hf == 0:
                        act.wait_ge(gain_ready, T("g", 1))
                    for k in range(KT):
                        i = hf * KT + k
                        act.wait_ge(tb_ready, T("b", i + 1))
                        reach(act, lo_done, T("h", i - 1))
                        nc.scalar.activation(TA[:, k % 2, :], TB[:, k % 2, :], ACT.Identity,
                                             scale=scale[:, k:k + 1],
                                             bias=0.0 if shift is None else shift[:, k:k + 1]).then_inc(ta_ready, 1)
                        act.wait_ge(ta_ready, T("t", i + 1))
                        nc.scalar.activation(Hhi[:, k, half(hf)], TA[:, k % 2, :], ACT.Copy).then_inc(hi_done, 1)

            def up(T, par, first):
                for hf in range(NH):
                    for f in range(FT):
                        i = hf * FT + f
                        act.wait_ge(a_ready, T("a", i + 1))
                        act.wait_ge(ta_ready, T("t", i - 1))
                        nc.scalar.activation(TB[:, i % 2, :], A[:, i % 2, :], ACT.Relu).then_inc(a_free, 1)
                        act.wait_ge(a_free, T("a", i + 1))
                        act.wait_ge(lo_done, T("h", i - 1))
                        nc.scalar.activation(TA[:, i % 2, :], TB[:, i % 2, :], ACT.Square).then_inc(ta_ready, 1)
                        act.wait_ge(ta_ready, T("t", i + 1))
                        nc.scalar.activation(Mhi[:, par, f, half(hf)], TA[:, i % 2, :], ACT.Copy).then_inc(hi_done, 1)

            def values(T, j):
                for i in range(KT):
                    act.wait_ge(a_ready, T("a", i + 1))
                    nc.scalar.activation(V[:, i, j * UC:(j + 1) * UC], A[:, i % 2, 0:UC], ACT.Gelu).then_inc(a_free, 1)

            def gates(T, j):
                for hf in range(NH):
                    for f in range(FT):
                        i = hf * FT + f
                        act.wait_ge(a_ready, T("a", i + 1))
                        act.wait_ge(x_stored, 16 * KT * T("sp"))
                        nc.scalar.activation(X[:, j * FT + f, half(hf)], A[:, i % 2, :], ACT.Gelu).then_inc(a_free, 1)

            def between(T, j):
                if j == 0:
                    act.wait_ge(v_norm, 1)
                    nc.scalar.activation(vstd[:], mv[:, :, 1], ACT.Sqrt, scale=1.0, bias=epsc[:, 1:2]).then_inc(v_std, 1)

            def mix(T, j):
                act.wait_ge(v_norm, 2)
                act.wait_ge(ws_masked, KT)
                act.wait_ge(row_sum, 1)
                reach(act, d_ready, T("d"))
                for h in range(2):
                    nc.scalar.activation(WShi[:, h, :], ws[:, 2 * j + h, :], ACT.Copy).then_inc(hi_done, 1)
                    nc.scalar.activation(Vhi[:, h], V[:, :, (2 * j + h) * P:(2 * j + h + 1) * P],
                                         ACT.Copy).then_inc(hi_done, 1)

            def resplit(T):
                if T("v") > 0:
                    act.wait_ge(mixed_done, T("vg"))
                act.wait_ge(d_free, T("d"))
                act.wait_ge(a_ready, T("a"))
                for k in range(KT):
                    nc.scalar.activation(Hhi[:, k, :], X[:, k, :], ACT.Copy).then_inc(hi_done, 1)

            def scale_x(T, name, source):
                for hf in range(NH):
                    squares(T, hf, source)

            def slot_for(T, i):
                slot = (T.n["o"] + i) % SLOTS
                stored = T.stored[slot] - (2 if i < 0 else 0)
                reach(act, slot_stored[slot], 16 * stored)
                return slot

            def heads(T, what, j, nf):
                for i in range(2 * nf):
                    r = T.n["r"] + i
                    act.wait_ge(a_ready, T("a", i + 1))
                    reach(act, qn_done, r - 1)
                    reach(act, ss_ready, r - 1)
                    if r < 2:
                        act.wait_ge(lo_done, T("h"))
                    nc.scalar.activation(TA[:, r % 2, :], A[:, i % 2, :], ACT.Copy).then_inc(head_copied, 1)
                    nc.scalar.activation(TB[:, r % 2, :], A[:, i % 2, :], ACT.Square).then_inc(a_free, 1)
                    head_std(r - 1)
                    head_hi(T, r - 2, i - 2)
                if what == "k":
                    head_std(r)
                    head_hi(T, r - 1, i - 1)
                    head_hi(T, r, i)

            def head_std(r):
                if r >= 0:
                    act.wait_ge(ss_ready, r + 1)
                    reach(act, qn_done, r - 1)
                    nc.scalar.activation(SQ[:, r % 2, :], B6, ACT.Sqrt, scale=1.0 / HD,
                                         bias=epsc[:, 0:1]).then_inc(sd_done, 1)

            def head_hi(T, r, i):
                if r >= 0:
                    act.wait_ge(rf_done, r + 1)
                    nc.scalar.activation(OH[:, slot_for(T, i), :], RF[:, r % 2, :], ACT.Copy).then_inc(out_hi, 1)

            def plain(T, what, head):
                for i in range(4):
                    slot = slot_for(T, i)
                    act.wait_ge(d_ready, T("d", i + 1))
                    nc.scalar.activation(OH[:, slot, :], Dn[:, i, :], ACT.Copy,
                                         scale=HD ** -0.5 if what == "q" else 1.0).then_inc(out_hi, 1)

            def vals(T, head, at, n):
                for i in range(QT):
                    slot = slot_for(T, i)
                    act.wait_ge(d_ready, T("d", i + 1))
                    nc.scalar.activation(OH[:, slot, 0:n], Dn[:, i % 4, 0:n], ACT.Copy).then_inc(out_hi, 1)

            def silu(T, j):
                for i in range(4):
                    slot = slot_for(T, i)
                    act.wait_ge(a_ready, T("a", i + 1))
                    nc.scalar.activation(OF[:, slot, :], A[:, i % 2, :], ACT.Silu).then_inc(a_free, 1)
                    act.wait_ge(a_free, T("a", i + 1))
                    nc.scalar.activation(OF[:, slot, 0:1], OF[:, slot, 0:1], ACT.Copy).then_inc(out_hi, 1)

            def exp(T, u, n):
                act.wait_ge(max_done, T("v", u + 1))
                reach(act, t_ready, T("v2", 2 * u - 2))
                scores = SB_[:, 2 * (u % 2):2 * (u % 2) + 2, :].rearrange("p b n -> p (b n)")[:, 0:n]
                nc.scalar.activation(PE_[:, u % 2, 0:n], scores, ACT.Exp, bias=neg_max[:, u % 4:u % 4 + 1],
                                     accum_out=den[:, u % 4:u % 4 + 1]).then_inc(exp_done, 1)

            def probs_hi(T, u, n):
                for g, first, m in banks(n):
                    act.wait_ge(t_ready, T("v2", 2 * u + g + 1))
                    if u % 4 == 0:
                        reach(act, o_ready, T("vg", u // 4 - 1))
                    nc.scalar.activation(probs_t(PTh, u, first, m), TP[:, g, 0:m * P]
                                         .rearrange("p (k q) -> p k q", q=P), ACT.Copy).then_inc(th_done, 1)

            def lower_half(T, g):
                act.wait_ge(o_ready, T("vg", g + 1))
                reach(act, os_done, T("vg", g - 1))
                nc.scalar.activation(OT[0:HD, g % 2, :], OB[HD:P, g % 2, :], ACT.Copy).then_inc(ot_done, 1)

            def attend(T, kind, i, before):
                for u in range(PAIR):
                    for w, k in lagged(u, 1, kind, before):
                        exp(T, w, width(k, w))
                    for w, k in lagged(u, 2, kind, before):
                        probs_hi(T, w, width(k, w))
                    for w, k in lagged(u, 7, kind, before):
                        if w % 4 == 0:
                            lower_half(T, w // 4)

            def attend_end(T):
                exp(T, -1, width("B", -1))
                for u in (-2, -1):
                    probs_hi(T, u, width("B", u))
                lower_half(T, -1)

            def nothing(T, *_):
                pass

            walk(act, dict(start=start, ada=nothing, mods=nothing, split=split, norm_pool=norm_pool, norm=norm,
                           pool=nothing, up=up, down=nothing, spill=nothing, values=values, gates=gates, between=between,
                           mix=mix, resplit=resplit, project=nothing, scale_x=scale_x, finish=nothing, heads=heads, vals=vals, silu=silu, plain=plain, attend_start=nothing, attend=attend,
                            attend_end=attend_end))

        @block.vector
        def _(dve):
            own = [0]

            def chained(instruction):
                own[0] += 1
                instruction.then_inc(dve_own, 1)
                dve.wait_ge(dve_own, own[0])

            def start(T):
                dve.wait_ge(c_ready, 1)

            def ada(T, l, cc, q):
                s = T.n["u"] % STAGES
                if q == 0:
                    reach(dve, ada_sum, T("mod"))
                dve.wait_ge(stage_in[s], T.fill() * 16)
                reach(dve, unit_done, T("u"))
                if q == 0:
                    nc.vector.tensor_scalar(out=acc[:], in0=stage[:, s, 0:D], scalar1=c_act[:, 0:1], scalar2=None,
                                            op0=ALU.mult).then_inc(ada_half, 1)
                else:
                    nc.vector.scalar_tensor_tensor(out=acc[:], in0=stage[:, s, 0:D], scalar=c_act[:, 2 * q:2 * q + 1],
                                                   in1=acc[:], op0=ALU.mult, op1=ALU.add).then_inc(ada_half, 1)
                dve.wait_ge(ada_half, T("ada", 1))
                nc.vector.scalar_tensor_tensor(out=acc[:], in0=stage[:, s, D:2 * D],
                                               scalar=c_act[:, 2 * q + 1:2 * q + 2], in1=acc[:], op0=ALU.mult,
                                               op1=ALU.add).then_inc(unit_done, 1)

            def mods(T, l, cc):
                dve.wait_ge(ada_sum, T("mod", 1))
                b = COLS[f"ada_b{l}"][0]
                nc.vector.tensor_tensor(mod[:, l, bass.ds(cc * KT, KT)], B6[:, 0:KT],
                                        cols[:, bass.ds(cc * KT + b, KT)], ALU.add).then_inc(mod_done, 1)

            def split(T, src):
                s, w = T.n["u"] % STAGES, T.n["w"] % 2
                dve.wait_ge(w_hi, T("w", 1))
                nc.vector.tensor_tensor(Wlo[:, w, :], stage[:, s, :], Whi[:, w, :].bitcast(F32),
                                        ALU.subtract).then_inc(unit_done, 1)

            def make_gain(T, which):
                l, sc = which // 2, (which % 2) * 3 * KT + KT
                dve.wait_ge(mod_done, T("mod"))
                nc.vector.scalar_tensor_tensor(out=gain[:, which, :], in0=mod[:, l, sc:sc + KT], scalar=1.0,
                                               in1=col(("mix_g", "mlp_g")[which % 2] + str(l)), op0=ALU.add,
                                               op1=ALU.mult).then_inc(gain_ready, 1)

            def invert(T, hf):
                dve.wait_ge(std_ready, T("n", hf + 1))
                reach(dve, diag_ready, T("n", hf))
                nc.vector.reciprocal(rstd[:], std[:]).then_inc(rstd_own, 1)
                dve.wait_ge(rstd_own, T("n", hf + 1))
                reach(dve, rstd_ready, T("n", hf))
                if T.n["n"] == 0:
                    dve.wait_ge(const_loaded, 16)
                for t in range(4):
                    ins = nc.vector.tensor_scalar(out=diag[:, t * P:(t + 1) * P], in0=con("ident"),
                                                  scalar1=rstd[:, t:t + 1], scalar2=None, op0=ALU.mult)
                ins.then_inc(diag_ready, 1)
                dve.wait_ge(rstd_ready, T("n", hf + 1))

            def norm_pool(T):
                for hf in range(NH):
                    invert(T, hf)
                make_gain(T, 0)
                dve.wait_ge(set_ready, 5)
                for k in range(KT):
                    for hf, bank in enumerate((B7, B6)):
                        reach(dve, ta_ready, T("t", 2 * k + hf - 1))
                        nc.vector.tensor_tensor(TB[:, hf, :], X[:, k, half(hf)], bank,
                                                ALU.mult).then_inc(tb_ready, 1)
                    dve.wait_ge(ta_ready, T("t", 2 * k + 2))
                    group, last, reach_back = k // 2, PH[:, k % 2, :], 1
                    for j in range(group + 1):
                        chained(nc.vector.tensor_tensor(PS[:, j % 2, PAD:], last[:, PAD:],
                                                        last[:, PAD - reach_back:PAD + S - reach_back], ALU.add))
                        last, reach_back = PS[:, j % 2, :], 2 * reach_back
                    if k >= 2:
                        dve.wait_ge(hi_done, T("h", k - 1))
                        dve.wait_ge(lo_done, T("h", k - 1))
                    chained(nc.vector.scalar_tensor_tensor(out=PO[:, k % 2, :], in0=last[:, PAD:],
                                                           scalar=1.0 / WINDOWS[group], in1=PH[:, k % 2, PAD:],
                                                           op0=ALU.mult, op1=ALU.subtract))
                    chained(nc.vector.tensor_tensor(PF[:], last[:, PAD:PAD + 16],
                                                    con("invc")[:, group * 16:(group + 1) * 16], ALU.mult))
                    nc.vector.tensor_tensor(PO[:, k % 2, 0:16], PF[:], PH[:, k % 2, PAD:PAD + 16],
                                            ALU.subtract).then_inc(po_ready, 1)
                    if k >= 1:
                        pooled_lo(T, k - 1)
                pooled_lo(T, KT - 1)

            def pooled_lo(T, k):
                dve.wait_ge(hi_done, T("h", k + 1))
                nc.vector.tensor_tensor(Hlo[:, k, :], PO[:, k % 2, :], Hhi[:, k, :].bitcast(F32),
                                        ALU.subtract).then_inc(lo_done, 1)

            def split_lo(T, i, out_lo, out_hi):
                dve.wait_ge(hi_done, T("h", i + 1))
                nc.vector.tensor_tensor(out_lo, TA[:, i % 2, :], out_hi.bitcast(F32),
                                        ALU.subtract).then_inc(lo_done, 1)

            def norm(T, which):
                if which < 4:
                    make_gain(T, which)
                for hf in range(NH):
                    invert(T, hf)
                    for k in range(KT + 1):
                        i = hf * KT + k
                        if k < KT:
                            dve.wait_ge(ta_ready, T("t", i - 1))
                            nc.vector.tensor_tensor(TB[:, k % 2, :], X[:, k, half(hf)], B7,
                                                    ALU.mult).then_inc(tb_ready, 1)
                        if k >= 1:
                            split_lo(T, i - 1, Hlo[:, k - 1, half(hf)], Hhi[:, k - 1, half(hf)])

            def up(T, par, first):
                for hf in range(NH):
                    for f in range(FT):
                        split_lo(T, hf * FT + f, Mlo[:, par, f, half(hf)], Mhi[:, par, f, half(hf)])

            def add_to_x(T, gate):
                for hf in range(NH):
                    for k in range(KT):
                        i = hf * KT + k
                        dve.wait_ge(d_ready, T("d", i + 1))
                        reach(dve, d_free, T("d", i - 15))
                        nc.vector.scalar_tensor_tensor(out=X[:, k, half(hf)], in0=Dn[:, i % D_BANKS, :],
                                                       scalar=gate[:, k:k + 1], in1=X[:, k, half(hf)],
                                                       op0=ALU.mult, op1=ALU.add).then_inc(d_free, 1)

            def pool(T):
                dve.wait_ge(mod_done, T("mod"))
                chained(nc.vector.tensor_tensor(pg[:], mod[:, 0, 2 * KT:3 * KT], col("pool_scale"), ALU.mult))
                add_to_x(T, pg)

            def down(T, gate, par, ahead):
                add_to_x(T, gate)

            def spill(T):
                if T("sp") == 0:
                    dve.wait_ge(ws_loaded, 32)
                    dve.wait_ge(row_sum, 1)
                    for h in range(KT):
                        bank = (B6, B7)[h // 4]
                        nc.vector.scalar_tensor_tensor(out=bs[:, h, :], in0=bank[:, h % 4 * P:(h % 4 + 1) * P],
                                                       scalar=col("ln_b")[:, h:h + 1], in1=bs[:, h, :],
                                                       op0=ALU.mult, op1=ALU.add).then_inc(bs_ready, 1)

            def between(T, j):
                if j == 0:
                    dve.wait_ge(a_free, T("a"))
                    for i in range(KT):
                        for b in range(2):
                            nc.vector.bn_stats(bstat[:, i, b, :], V[:, i, b * H:(b + 1) * H]).then_inc(bs_own, 1)
                    for i in range(KT):
                        dve.wait_ge(bs_own, 2 * i + 2)
                        ins = nc.vector.bn_aggr(mv[:, i, :], bstat[:, i].rearrange("p b s -> p (b s)"))
                    ins.then_inc(v_norm, 1)
                if j == 1:
                    dve.wait_ge(v_std, 1)
                    chained(nc.vector.reciprocal(vrs[:], vstd[:]))
                    for i in range(KT):
                        ins = nc.vector.tensor_scalar(out=V[:, i, :], in0=V[:, i, :], scalar1=mv[:, i, 0:1],
                                                      scalar2=vrs[:, i:i + 1], op0=ALU.subtract, op1=ALU.mult)
                    ins.then_inc(v_norm, 1)

            def mix(T, j):
                for h in range(2):
                    dve.wait_ge(hi_done, T("h", 2 * h + 1))
                    nc.vector.tensor_tensor(WSlo[:, h, :], ws[:, 2 * j + h, :], WShi[:, h, :].bitcast(F32),
                                            ALU.subtract).then_inc(lo_done, 1)
                    dve.wait_ge(hi_done, T("h", 2 * h + 2))
                    nc.vector.tensor_tensor(Vlo[:, h], V[:, :, (2 * j + h) * P:(2 * j + h + 1) * P],
                                            Vhi[:, h].bitcast(F32), ALU.subtract).then_inc(lo_done, 1)
                for h in range(2):
                    head = 2 * j + h
                    for hf in range(NH):
                        i = 2 * h + hf
                        dve.wait_ge(d_ready, T("d", i + 1))
                        dve.wait_ge(a_free, T("a"))
                        dve.wait_ge(bs_ready, KT)
                        bank = Dn[:, i % D_BANKS, :]
                        chained(nc.vector.scalar_tensor_tensor(
                            out=bank.rearrange("p (n t) -> p n t", t=P), in0=bank.rearrange("p (n t) -> p n t", t=P),
                            scalar=col("ln_g")[:, head:head + 1],
                            in1=bs[:, head:head + 1, :].broadcast_to([P, 4, P]), op0=ALU.mult, op1=ALU.add))
                        nc.vector.tensor_tensor(X[:, head, half(hf)], bank, X[:, head, half(hf)],
                                                ALU.mult).then_inc(d_free, 1)

            def resplit(T):
                for k in range(KT):
                    dve.wait_ge(hi_done, T("h", k + 1))
                    nc.vector.tensor_tensor(Hlo[:, k, :], X[:, k, :], Hhi[:, k, :].bitcast(F32),
                                            ALU.subtract).then_inc(lo_done, 1)

            def project(T, j, gate, first):
                if first:
                    dve.wait_ge(x_back, 16 * KT * T("sp"))
                for i in range(4):
                    hf, k = i // 2, FT * j + i % 2
                    dve.wait_ge(d_ready, T("d", i + 1))
                    nc.vector.scalar_tensor_tensor(out=X[:, k, half(hf)], in0=Dn[:, i, :], scalar=gate[:, k:k + 1],
                                                   in1=X[:, k, half(hf)], op0=ALU.mult, op1=ALU.add).then_inc(d_free, 1)

            def heads(T, what, j, nf):
                if T.n["r"] == 0:
                    chained(nc.vector.tensor_scalar(out=qg8[:, 0:1], in0=col("qg"), scalar1=HD ** -0.5, scalar2=None,
                                                    op0=ALU.mult))
                    dve.wait_ge(rope_loaded, 16)
                for i in range(2 * nf):
                    r = T.n["r"] + i
                    head_norm(r - 1)
                    head_rope(T, r - 2, half_of(r - 2), i - 2)
                if what == "k":
                    head_norm(r)
                    head_rope(T, r - 1, half_of(r - 1), i - 1)
                    head_rope(T, r, half_of(r), i)

            def half_of(r):
                return r % 4 // 2 if r < 8 else r - 8

            def head_norm(r):
                if r >= 0:
                    g = qg8[:, 0:1] if r < 8 else col("kg")
                    dve.wait_ge(sd_done, r + 1)
                    dve.wait_ge(head_copied, r + 1)
                    chained(nc.vector.reciprocal(SQ[:, r % 2, :], SQ[:, r % 2, :]))
                    reach(dve, rot_ready, r - 1)
                    nc.vector.scalar_tensor_tensor(out=QN[:, r % 2, :], in0=TA[:, r % 2, :], scalar=g,
                                                   in1=SQ[:, r % 2, :], op0=ALU.mult, op1=ALU.mult).then_inc(qn_done, 1)

            def head_rope(T, r, hf, i):
                if r >= 0:
                    dve.wait_ge(qn_done, r + 1)
                    chained(nc.vector.tensor_tensor(RT[:, 0, :], QN[:, r % 2, :], rope[:, 0, half(hf)], ALU.mult))
                    dve.wait_ge(rot_ready, r + 1)
                    chained(nc.vector.tensor_tensor(RT[:, 1, :], B7, rope[:, 1, half(hf)], ALU.mult))
                    nc.vector.tensor_tensor(RF[:, r % 2, :], RT[:, 0, :], RT[:, 1, :], ALU.add).then_inc(rf_done, 1)
                    slot = (T.n["o"] + i) % SLOTS
                    dve.wait_ge(out_hi, T("o", i + 1))
                    nc.vector.tensor_tensor(OL[:, slot, :], RF[:, r % 2, :], OH[:, slot, :].bitcast(F32),
                                            ALU.subtract).then_inc(out_lo, 1)

            def plain(T, what, head):
                for i in range(4):
                    slot = (T.n["o"] + i) % SLOTS
                    dve.wait_ge(out_hi, T("o", i + 1))
                    nc.vector.scalar_tensor_tensor(out=OL[:, slot, :], in0=Dn[:, i, :],
                                                   scalar=HD ** -0.5 if what == "q" else 1.0,
                                                   in1=OH[:, slot, :].bitcast(F32), op0=ALU.mult,
                                                   op1=ALU.subtract).then_inc(d_free, 1)
                    out_lo_too(T, i, slot)

            def out_lo_too(T, i, slot):
                dve.wait_ge(d_free, T("d", i + 1))
                nc.vector.tensor_copy(OL[:, slot, 0:1], OL[:, slot, 0:1].bitcast(F32)).then_inc(out_lo, 1)

            def vals(T, head, at, n):
                for i in range(QT):
                    slot = (T.n["o"] + i) % SLOTS
                    dve.wait_ge(out_hi, T("o", i + 1))
                    nc.vector.tensor_tensor(OL[:, slot, 0:n], Dn[:, i % 4, 0:n], OH[:, slot, 0:n].bitcast(F32),
                                            ALU.subtract).then_inc(d_free, 1)
                    out_lo_too(T, i, slot)

            def row_maxima(T, u, kind, n):
                dve.wait_ge(s_ready, T("v", u + 1))
                at = u % 4
                scores = SB_[:, 2 * (u % 2):2 * (u % 2) + 2, :].rearrange("p b n -> p (b n)")[:, 0:n]
                reach(dve, exp_done, T("v", u - 3))
                if kind == "A":
                    nc.vector.tensor_reduce(neg_max[:, at:at + 1], scores, AX_X, ALU.max, negate=True) \
                        .then_inc(max_done, 1)
                    return
                if u % QT == 0:
                    dve.wait_ge(bias_masked, T.masked(u // QT))
                first, rows = neighbourhood(u % QT)
                b0 = (first - 2 * (u % QT) + 6) * GRID if rows == NKH else NF
                nc.vector.tensor_tensor(scores, scores, bias[:, u // QT, b0:b0 + n], ALU.add).then_inc(max_own, 1)
                dve.wait_ge(max_own, T.b_units(u + 1))
                nc.vector.tensor_reduce(neg_max[:, at:at + 1], scores, AX_X, ALU.max, negate=True).then_inc(max_done, 1)

            def invert_sum(T, u):
                dve.wait_ge(exp_done, T("v", u + 1))
                reach(dve, rd_done, T("v", u - 3))
                nc.vector.reciprocal(rden[:, u % 4:u % 4 + 1], den[:, u % 4:u % 4 + 1]).then_inc(rd_own, 1)
                dve.wait_ge(rd_own, T("v", u + 1))
                reach(dve, t_ready, T("v2", 2 * u - 2))
                nc.vector.tensor_scalar(out=DG[:, u % 2, :], in0=con("ident"), scalar1=rden[:, u % 4:u % 4 + 1],
                                        scalar2=None, op0=ALU.mult).then_inc(rd_done, 1)

            def probs_lo(T, u, n):
                for g, first, m in banks(n):
                    dve.wait_ge(th_done, T("v2", 2 * u + g + 1))
                    nc.vector.tensor_tensor(probs_t(PTl, u, first, m),
                                            TP[:, g, 0:m * P].rearrange("p (k q) -> p k q", q=P),
                                            probs_t(PTh, u, first, m).bitcast(F32), ALU.subtract).then_inc(tl_done, 1)

            def gated(T, g, tile):
                e = g // 2 % 2
                part, hf = slice(e * HD, (e + 1) * HD), g % 2
                dve.wait_ge(ot_done, T("vg", g + 1))
                reach(dve, mixed_done, T("vg", g - 1))
                nc.vector.tensor_tensor(OS[part, g % 2, :], OB[0:HD, g % 2, :], OT[0:HD, g % 2, :],
                                        ALU.add).then_inc(os_done, 1)
                dve.wait_ge(os_done, T("vg", g + 1))
                dst = X[part, bass.ds(tile, 1), half(hf)].rearrange("p a n -> p (a n)")
                nc.vector.tensor_tensor(dst, OS[part, g % 2, :], dst, ALU.mult).then_inc(mixed_done, 1)

            def attend(T, kind, i, before):
                if kind == "A" and before is None:
                    dve.wait_ge(gates_loaded, 16 * KT)
                for u in range(PAIR):
                    row_maxima(T, u, kind, width(kind, u))
                    for w, k in lagged(u, 1, kind, before):
                        invert_sum(T, w)
                    for w, k in lagged(u, 2, kind, before):
                        probs_lo(T, w, width(k, w))
                    for w, k in lagged(u, 7, kind, before):
                        if w % 4 == 0:
                            gated(T, w // 4, tile_of(kind, i, w < 0))

            def tile_of(kind, i, previous):
                return i + (4 if kind == "B" else 0) - (1 if previous else 0)

            def attend_end(T):
                invert_sum(T, -1)
                for u in (-2, -1):
                    probs_lo(T, u, width("B", u))
                gated(T, -1, KT - 1)

            def scale_x(T, name, source):
                for hf in range(NH):
                    invert(T, hf)
                    for k in range(KT):
                        nc.vector.scalar_tensor_tensor(out=X[:, k, half(hf)], in0=X[:, k, half(hf)],
                                                       scalar=col(name)[:, k:k + 1], in1=B7, op0=ALU.mult,
                                                       op1=ALU.mult).then_inc(x_scaled, 1)

            def nothing(T, *_):
                pass

            walk(dve, dict(start=start, ada=ada, mods=mods, split=split, norm_pool=norm_pool, norm=norm,
                           pool=pool, up=up, down=down, spill=spill, values=nothing, gates=nothing, between=between,
                           mix=mix, resplit=resplit, project=project, scale_x=scale_x, finish=nothing, heads=heads, vals=vals, silu=nothing, plain=plain, attend_start=nothing, attend=attend,
                            attend_end=attend_end))

        @block.tensor
        def _(pe):
            def product(out_bank, hi_lo_w, hi_lo_x, start, stop):
                (whi, wlo), (xhi, xlo) = hi_lo_w, hi_lo_x
                nc.tensor.matmul(out_bank, whi, xhi, start=start, stop=False)
                nc.tensor.matmul(out_bank, whi, xlo, start=False, stop=False)
                return nc.tensor.matmul(out_bank, wlo, xhi, start=False, stop=stop)

            def weights(T, at):
                c = T.n["c"] % 2
                return Whi[:, c, at:at + P], Wlo[:, c, at:at + P]

            def start(T):
                pe.wait_ge(set_ready, 5)

            def ada(T, l, cc, q):
                pass

            def mods(T, l, cc):
                pe.wait_ge(unit_done, T("u"))
                reach(pe, mod_done, T("mod"))
                for j in range(KT):
                    ins = nc.tensor.matmul(B6[:, j:j + 1], acc[:, j * P:(j + 1) * P], ones[:, 0:1],
                                           start=True, stop=True)
                ins.then_inc(ada_sum, 1)

            def stat(T, hf):
                pe.wait_ge(sum_done, T("s", 7 * hf + 7))
                for t in range(4):
                    ins = nc.tensor.matmul(B6[:, t:t + 1], SUM[:, t * P:(t + 1) * P], ones[:, 0:1],
                                           start=True, stop=True)
                ins.then_inc(stat_ready, 1)

            def spread(T, hf, bank):
                pe.wait_ge(diag_ready, T("n", hf + 1))
                nc.tensor.matmul(bank, ones[:], diag[:], start=True, stop=True).then_inc(rstd_ready, 1)

            def norm_pool(T):
                reach(pe, mod_done, T("mod"))
                stat(T, 0)
                pe.wait_ge(diag_ready, T("n", 1))
                nc.tensor.matmul(B7, ones[:], diag[:], start=True, stop=True).then_inc(rstd_ready, 1)
                stat(T, 1)
                pe.wait_ge(diag_ready, T("n", 2))
                nc.tensor.matmul(B6[:], ones[:], diag[:], start=True, stop=True).then_inc(rstd_ready, 1)

            def norm(T, which, reader="tb_ready"):
                reach(pe, mod_done, T("mod"))
                for hf in range(NH):
                    if reader == "tb_ready":
                        pe.wait_ge(tb_ready, T("b", KT * hf))
                    if reader == "x_scaled" or hf == 0:
                        reach(pe, x_scaled, T("x", KT * hf if reader == "x_scaled" else 0))
                    if hf == 0 and which == 3:
                        pe.wait_ge(bs_ready, KT)
                    stat(T, hf)
                    spread(T, hf, B7)

            def pool(T):
                pe.wait_ge(unit_done, T("uc"))
                for hf in range(NH):
                    for k in range(KT):
                        i, g, d = hf * KT + k, k // 2, k % 2
                        reach(pe, d_free, T("d", i - D_BANKS + 1))
                        for kk in range(2):
                            pe.wait_ge(lo_done, 2 * g + kk + 1)
                            ins = product(Dn[:, i % D_BANKS, :], weights(T, (2 * g + kk) * 2 * P + d * P),
                                          (Hhi[:, 2 * g + kk, half(hf)], Hlo[:, 2 * g + kk, half(hf)]),
                                          kk == 0, kk == 1)
                        ins.then_inc(d_ready, 1)

            def up(T, par, first=False):
                pe.wait_ge(unit_done, T("uc"))
                for hf in range(NH):
                    for f in range(FT):
                        i = hf * FT + f
                        reach(pe, a_free, T("a", i - A_BANKS + 1))
                        for k in range(KT):
                            if first and f == 0:
                                pe.wait_ge(lo_done, T("h", hf * KT + k + 1 - 2 * KT))
                            ins = product(A[:, i % A_BANKS, :], weights(T, k * UC + f * P),
                                          (Hhi[:, k, half(hf)], Hlo[:, k, half(hf)]), k == 0, k == KT - 1)
                        ins.then_inc(a_ready, 1)

            def down(T, gate, par, ahead):
                pe.wait_ge(unit_done, T("uc"))
                for hf in range(NH):
                    for k in range(KT):
                        i = hf * KT + k
                        reach(pe, d_free, T("d", i - D_BANKS + 1))
                        for f in range(FT):
                            if i == 0:
                                pe.wait_ge(lo_done, T("h", -ahead))
                            ins = product(Dn[:, i % D_BANKS, :], weights(T, f * D + k * P),
                                          (Mhi[:, par, f, half(hf)], Mlo[:, par, f, half(hf)]), f == 0, f == FT - 1)
                        ins.then_inc(d_ready, 1)

            def spill(T):
                if T("sp") == 0:
                    pe.wait_ge(ws_masked, KT)
                    pe.wait_ge(tb_ready, T("b"))
                    for g, bank in enumerate((B6, B7)):
                        ins = nc.tensor.matmul(bank, ones[:], ws[:, 4 * g:4 * g + 4, :], start=True, stop=True)
                    ins.then_inc(row_sum, 1)

            def values(T, j):
                pe.wait_ge(unit_done, T("uc"))
                c = T.n["c"] % 2
                for i in range(KT):
                    reach(pe, a_free, T("a", i - A_BANKS + 1))
                    for k in range(KT):
                        if j == 0:
                            pe.wait_ge(lo_done, T("h", KT * (i // 4) + k + 1 - 2 * KT))
                        tok = slice(i * P, (i + 1) * P)
                        out_bank, w = A[:, i % A_BANKS, 0:UC], slice(k * UC, (k + 1) * UC)
                        nc.tensor.matmul(out_bank, Hhi[:, k, tok], Whi[:, c, w], start=k == 0, stop=False)
                        nc.tensor.matmul(out_bank, Hhi[:, k, tok], Wlo[:, c, w], start=False, stop=False)
                        ins = nc.tensor.matmul(out_bank, Hlo[:, k, tok], Whi[:, c, w], start=False, stop=k == KT - 1)
                    ins.then_inc(a_ready, 1)

            def mix(T, j):
                for h in range(2):
                    pe.wait_ge(lo_done, T("h", 2 * h + 2))
                    for hf in range(NH):
                        i = 2 * h + hf
                        reach(pe, d_free, T("d", i - D_BANKS + 1))
                        for n in range(4):
                            ins = product(Dn[:, i, n * P:(n + 1) * P], (Vhi[:, h, 4 * hf + n, :], Vlo[:, h, 4 * hf + n, :]),
                                          (WShi[:, h, :], WSlo[:, h, :]), True, True)
                        ins.then_inc(d_ready, 1)

            def project(T, j, gate, first):
                pe.wait_ge(unit_done, T("uc"))
                for i in range(4):
                    hf, f = i // 2, i % 2
                    reach(pe, d_free, T("d", i - D_BANKS + 1))
                    for k in range(KT):
                        if first and i == 0:
                            pe.wait_ge(lo_done, T("h", k + 1 - KT))
                        ins = product(Dn[:, i, :], weights(T, k * UC + f * P),
                                      (Hhi[:, k, half(hf)], Hlo[:, k, half(hf)]), k == 0, k == KT - 1)
                    ins.then_inc(d_ready, 1)

            def scale_x(T, name, source):
                norm(T, None, "x_scaled")

            def heads(T, what, j, nf):
                pe.wait_ge(unit_done, T("uc"))
                for i in range(2 * nf):
                    hf, f, r = i // nf, i % nf, T.n["r"] + i
                    reach(pe, a_free, T("a", i - A_BANKS + 1))
                    for k in range(KT):
                        if r == 0 or (r == 2):
                            pe.wait_ge(lo_done, T("h", hf * KT + k + 1 - 2 * KT))
                        ins = product(A[:, i % A_BANKS, :], weights(T, k * UC + f * P),
                                      (Hhi[:, k, half(hf)], Hlo[:, k, half(hf)]), k == 0, k == KT - 1)
                    ins.then_inc(a_ready, 1)
                    head_sum(T, r - 1)
                    rotate(r - 2)
                if what == "k":
                    head_sum(T, r)
                    rotate(r - 1)
                    rotate(r)

            def head_sum(T, r):
                if r >= 0:
                    pe.wait_ge(a_free, r + 1 + T.n["a"] - T.n["r"])
                    reach(pe, sd_done, r)
                    nc.tensor.matmul(B6, con("pairs"), TB[:, r % 2, :], start=True, stop=True).then_inc(ss_ready, 1)

            def rotate(r):
                if r >= 0:
                    pe.wait_ge(qn_done, r + 1)
                    reach(pe, rf_done, r)
                    nc.tensor.matmul(B7, con("rot"), QN[:, r % 2, :], start=True, stop=True).then_inc(rot_ready, 1)

            def plain(T, what, head):
                project(T, 0, None, False)

            def vals(T, head, at, n):
                pe.wait_ge(unit_done, T("uc"))
                c = T.n["c"] % 2
                for i in range(QT):
                    reach(pe, d_free, T("d", i - D_BANKS + 1))
                    tok, bank = slice(i * P, (i + 1) * P), Dn[:, i % D_BANKS, 0:n]
                    for k in range(KT):
                        w = slice(k * UC + at, k * UC + at + n)
                        nc.tensor.matmul(bank, Hhi[:, k, tok], Whi[:, c, w], start=k == 0, stop=False)
                        nc.tensor.matmul(bank, Hhi[:, k, tok], Wlo[:, c, w], start=False, stop=False)
                        ins = nc.tensor.matmul(bank, Hlo[:, k, tok], Whi[:, c, w], start=False, stop=k == KT - 1)
                    ins.then_inc(d_ready, 1)

            def scores(T, u, kind, n):
                e, qt = u // QT, u % QT
                k0 = 0 if kind == "A" else neighbourhood(qt)[0] * GRID
                if qt == 0:
                    pe.wait_ge(qk_loaded[e], T.loads(6 * 16))
                    pe.wait_ge(v_loaded[e], T.loads(2 * 16))
                reach(pe, exp_done, T("v", u - 1))
                for at in range(0, n, H):
                    m = min(H, n - at)
                    bank = SB_[:, 2 * (u % 2) + at // H, 0:m]
                    q = QS[:, e, qt * P:(qt + 1) * P]
                    nc.tensor.matmul(bank, q, KH[:, e, k0 + at:k0 + at + m], start=True, stop=False)
                    ins = nc.tensor.matmul(bank, q, KL[:, e, k0 + at:k0 + at + m], start=False, stop=True)
                ins.then_inc(s_ready, 1)

            def turn(T, u, n):
                pe.wait_ge(rd_done, T("v", u + 1))
                for g, first, m in banks(n):
                    reach(pe, tl_done, T("v2", 2 * u + g - 1))
                    for k in range(m):
                        a = (first + k) * P
                        part = min(P, n - a)
                        ins = nc.tensor.matmul(TP[0:part, g, k * P:(k + 1) * P], PE_[:, u % 2, a:a + part],
                                               DG[:, u % 2, :], start=True, stop=True)
                    ins.then_inc(t_ready, 1)

            def outputs(T, g, kind):
                e = g // 2 % 2
                pe.wait_ge(tl_done, T("v2", 8 * g + 8))
                reach(pe, os_done, T("vg", g - 1))
                v = PTh, PTl
                if kind == "A":
                    for k in range(QT):
                        for x in v:
                            ins = nc.tensor.matmul(OB[:, g % 2, :], VT[:, e, k, :], x[:, g % 2, k, :],
                                                   start=k == 0 and x is v[0], stop=k == QT - 1 and x is v[1])
                else:
                    for t in range(4):
                        qt = g % 2 * 4 + t
                        first, rows = neighbourhood(qt)
                        n = rows * GRID
                        tiles = (n + P - 1) // P
                        for k in range(tiles):
                            part = min(P, n - k * P)
                            for x in v:
                                ins = nc.tensor.matmul(OB[:, g % 2, t * P:(t + 1) * P],
                                                       VT[0:part, e, first // 2 + k, :],
                                                       x[0:part, g % 2, k, t * P:(t + 1) * P],
                                                       start=k == 0 and x is v[0],
                                                       stop=k == tiles - 1 and x is v[1])
                ins.then_inc(o_ready, 1)

            def attend(T, kind, i, before):
                for u in range(PAIR):
                    scores(T, u, kind, width(kind, u))
                    for w, k in lagged(u, 2, kind, before):
                        turn(T, w, width(k, w))
                    for w, k in lagged(u, 6, kind, before):
                        if w % 4 == 0:
                            outputs(T, w // 4, k)

            def attend_end(T):
                for u in (-2, -1):
                    turn(T, u, width("B", u))
                outputs(T, -1, "B")

            def nothing(T, *_):
                pass

            walk(pe, dict(start=start, ada=ada, mods=mods, split=nothing, norm_pool=norm_pool, norm=norm,
                          pool=pool, up=up, down=down, spill=spill, values=values, gates=up, between=nothing, mix=mix,
                          resplit=nothing, project=project, scale_x=scale_x, finish=nothing, heads=heads, vals=vals, silu=lambda T, j: up(T, 0), plain=plain, attend_start=nothing, attend=attend,
                            attend_end=attend_end))


def pack_cols(vectors):
    return np.concatenate([np.ascontiguousarray(v.reshape(-1, P).T) for v in vectors], axis=1)


def constants():
    ident = np.eye(P, dtype=np.float32)
    tri = np.triu(np.ones((P, P), np.float32))
    pairs = np.kron(np.eye(2, dtype=np.float32), np.ones((64, 64), np.float32))
    rot = np.zeros((P, P), np.float32)
    for b in range(4):
        for j in range(16):
            rot[32 * b + 16 + j, 32 * b + j] = -1.0
            rot[32 * b + j, 32 * b + 16 + j] = 1.0
    invc = np.zeros((P, 4, 16), np.float32)
    for g, w in enumerate(WINDOWS):
        invc[:, g, :] = 1.0 / np.minimum(np.arange(16, dtype=np.float32) + 1, w)
    return np.concatenate([ident, tri, pairs, rot, invc.reshape(P, 64)], axis=1)


def rope_tables():
    t = np.arange(S)
    inv = np.float32(10000.0) ** (-np.arange(16, dtype=np.float32) * np.float32(2.0 / 32))
    row = (t // GRID).astype(np.float32)[:, None] * inv
    column = (t % GRID).astype(np.float32)[:, None] * inv
    ang = np.concatenate([row, row, column, column] * 2, axis=1).T
    return np.stack([np.cos(ang), np.sin(ang)]).astype(np.float32)


def masks():
    c = np.arange(GRID)
    start = np.clip(c - NKW // 2, 0, GRID - NKW)
    valid = (c[None, :] >= start[:, None]) & (c[None, :] < start[:, None] + NKW)
    full = np.tile(valid[None, :, None, :], (2, 1, 14, 1))
    inner = np.tile(valid[None, :, None, :], (2, 1, 9, 1))
    inner[0, :, 8] = False
    inner[1, :, 0] = False
    both = np.concatenate([full.reshape(P, -1), inner.reshape(P, -1)], axis=1)
    return np.where(both, np.float32(0), np.float32(-1e30))


def kernel(**inputs):
    import concourse.bacc as bacc
    from concourse.bass_utils import run_bass_kernel_spmd

    g = {k: np.asarray(v) for k, v in inputs.items()}
    two = lambda v: np.concatenate([v.reshape(-1), v.reshape(-1)])
    arrays = {
        "x_t": g["x"][0].T,
        "cols": pack_cols([g["c"], g["ada_b"][0], g["ada_b"][1], g["norm_mix_g"][0], g["norm_mix_g"][1],
                           g["norm_mlp_g"][0], g["norm_mlp_g"][1], g["pool_scale"], g["sgu_ln_g"], g["sgu_ln_b"],
                           g["final_g"], g["norm_gain_2"], g["final_norm_gain_2"], two(g["q_norm_a_2"]),
                           two(g["k_norm_a_2"])]),
        "const": constants(),
        "ada_w": g["ada_w"],
        "pool_w": g["pool_w"][0],
        "sgu_in": g["sgu_w_in"][0],
        "sgu_ws": g["sgu_w_s"][0].transpose(0, 2, 1),
        "sgu_bs": g["sgu_b_s"].reshape(1, -1),
        "sgu_out": g["sgu_w_out"][0],
        "w1": g["mlp_w1"],
        "w2": g["mlp_w2"],
        "rope": rope_tables(),
        "mask": masks(),
        "w_in2": g["w_in_2"][0],
        "rpb": np.pad(g["na_rpb_2"][0], ((0, 0), (0, 0), (48, 48))),
        "w_out2": g["w_out_2"][0],
    }
    arrays = {k: np.ascontiguousarray(v) for k, v in arrays.items()}
    nc = bacc.Bacc("TRN2", target_bir_lowering=False, num_devices=1, dynamic_dma_scratch_size=1024)
    args = [nc.dram_tensor(k, v.shape, mybir.dt.from_np(v.dtype), kind="ExternalInput").ap() for k, v in arrays.items()]
    out = nc.dram_tensor("out_t", (D, S), F32, kind="ExternalOutput").ap()
    build(nc, *args, out)
    r = run_bass_kernel_spmd(nc, [arrays], core_ids=[0])
    return np.ascontiguousarray(r.results[0]["out_t"].T)[None]
```

```python
import concourse.bass as bass
import numpy as np
from concourse import mybir

F32 = mybir.dt.float32
F32R = mybir.dt.float32r
ALU = mybir.AluOpType
ACT = mybir.ActivationFunctionType
AX_X = mybir.AxisListType.X

P = 128
S = 1024
D = 1024
KT = D // P
NH = 2
H = S // NH
F = 4 * D
UC = 256
UNIT = KT * UC
CHUNKS = F // UC
FT = UC // P
MODS = 6 * KT
STAGES = 4
A_BANKS, D_BANKS = 2, 4
WINDOWS = (2, 4, 8, 16)
HD = 64
QT = S // P
GRID = 64
ROWS = S // GRID
NKH, NKW = 8, 16
SLOTS = 8
PAIR = 2 * QT
LOADED = "a unit that SyncE has loaded already"
EPS = 1e-6
LN_EPS = 1e-5

COLS = {}
_at = 0
for _name, _n in (("c", KT), ("ada_b0", MODS), ("ada_b1", MODS), ("mix_g0", KT), ("mix_g1", KT),
                  ("mlp_g0", KT), ("mlp_g1", KT), ("pool_scale", KT), ("ln_g", KT), ("ln_b", KT),
                  ("final_g", KT), ("gain2", KT), ("final2", KT), ("qg", 1), ("kg", 1)):
    COLS[_name] = (_at, _at + _n)
    _at += _n
NCOLS = _at

def neighbourhood(qt):
    first = [min(max(r - NKH // 2, 0), ROWS - NKH) for r in (2 * qt, 2 * qt + 1)]
    return first[0], first[1] + NKH - first[0]


CONST = {}
_at = 0
for _name, _n in (("ident", P), ("tri", P), ("pairs", P), ("rot", P), ("invc", 4 * 16)):
    CONST[_name] = (_at, _at + _n)
    _at += _n
NCONST = _at


STEPS = ("start prepare ahead split ada mods norm_pool norm pool up down values normalise_v spatial gates mix "
         "resplit spill project scale_x rotation heads v_a silu plain vals attend_start attend attend_end "
         "finish").split()

LOAD_AT = {1: "q", 2: "kh", 3: "kl", 4: "bias", 7: "v"}


class Tally:

    def __init__(self):
        self.n = dict.fromkeys("u w c uc un a d t h b q s st n sp ada mod x g o ol r v v2 vg".split(), 0)
        self.reg, self.per = None, {}
        self.lead = 0
        self.stored = [0] * SLOTS

    def __call__(self, name, more=0):
        v = self.n[name] + more
        return self.reg * self.per[name] + v if self.reg is not None and self.per.get(name) else v

    def add(self, **more):
        for name, k in more.items():
            self.n[name] += k

    def b_units(self, u):
        return self("v", u - 4 * PAIR)

    def masked(self, e):
        v = (self.n["v"] // PAIR - 4) * 2 + e + 1
        return self.reg * 2 + v if self.reg is not None else v

    def loads(self, n, first=0, ahead=0):
        v = (self.n["v"] // PAIR + 1 + ahead - first) * n
        return self.reg * (self.per["v"] // PAIR * n) + v if self.reg is not None else v

    def fill(self):
        v = self.n["u"] // STAGES + 1
        return self.reg * (self.per["u"] // STAGES) + v if self.reg is not None else v

    def loop(self, eng, count, per, body):
        start = dict(self.n)
        with eng.Fori(0, count) as i:
            self.reg, self.per = i, per
            body(i)
            self.reg = None
        for name in self.n:
            assert name == "uc" or self.n[name] == start[name] + per.get(name, 0), name
            self.n[name] = start[name] + count * per.get(name, 0)


def reach(eng, sem, count):
    if not isinstance(count, int) or count > 0:
        eng.wait_ge(sem, count)



def build(nc, x_in, cols_in, const_in, ada_w, pool_w, sgu_in, sgu_ws, sgu_bs, sgu_out, w1, w2,
          rope_in, mask_in, w_in2, rpb, w_out2, out):
    top = [(nc.sbuf_base + 31) // 32 * 32]

    def sb(name, shape, dt=F32, at=None):
        size = 4 * int(np.prod(shape[1:]))
        where = top[0] if at is None else at
        if at is None:
            top[0] += (size + 31) // 32 * 32
        assert where + size <= nc.sbuf_usable_end, name
        return nc.alloc_sbuf_tensor_at(name, shape, dt, offset=where)

    cols = sb("cols", [P, NCOLS])
    const = sb("const", [P, NCONST])
    ones = sb("ones", [P, P])
    epsc = sb("epsc", [P, 3])
    c_act = sb("c_act", [P, KT])
    mod = sb("mod", [P, 2, MODS])
    gain = sb("gain", [P, 5, KT])
    pg = sb("pg", [P, KT])
    std = sb("std", [P, 4])
    std1 = sb("std1", [P, NH, 4])
    both = sb("both", [P, 4])
    g_sq = sb("g_sq", [P, KT, 2])
    rstd = sb("rstd", [P, 4])
    x_at = top[0]
    X = sb("X", [P, KT, S])
    h_at = top[0]
    Hhi = sb("Hhi", [P, KT, S], F32R)
    Hlo = sb("Hlo", [P, KT, S], F32R)
    m_at = top[0]
    Mhi = sb("Mhi", [P, 2, FT, S], F32R)
    Mlo = sb("Mlo", [P, 2, FT, S], F32R)
    Whi = sb("Whi", [P, 2, UNIT], F32R)
    Wlo = sb("Wlo", [P, 2, UNIT], F32R)
    stage = sb("stage", [P, STAGES, UNIT])
    t_at = top[0]
    TA = sb("TA", [P, 2, H])
    TB = sb("TB", [P, 2, H])
    SQ = sb("SQ", [P, 2, H])
    NB = sb("NB", [P, 4, H], at=t_at)
    diag = sb("diag", [P, H])
    SUM = sb("SUM", [P, H])
    acc_at = top[0]
    acc = sb("acc", [P, D])
    SUM2 = sb("SUM2", [P, H], at=m_at)
    Vhi = sb("Vhi", [P, 2, KT, P], F32R, at=t_at)
    Vlo = sb("Vlo", [P, 2, KT, P], F32R, at=t_at + 4 * 2 * S)
    ws = sb("ws", [P, KT, P], at=acc_at)
    bs = sb("bs", [P, KT, P])
    WShi = sb("WShi", [P, 2, P], F32R)
    WSlo = sb("WSlo", [P, 2, P], F32R)
    V = sb("V", [P, KT, D], at=m_at)
    bstat = sb("bstat", [P, KT, 2, 6], at=t_at)
    mv = sb("mv", [P, KT, 2])
    vstd = sb("vstd", [P, KT])
    vrs = sb("vrs", [P, KT])
    w_at = m_at + 32 * S
    rows = [sb(f"rows{pair}", [1, 2, D], at=where)
            for pair, where in enumerate((w_at + 4 * UNIT, w_at + 12 * UNIT, acc_at))]
    PW = sb("PW", [P, UNIT], at=acc_at)
    XN = sb("XN", [P, KT, S], at=x_at + 8 * KT * S)
    PAD = 16
    PH = sb("PH", [P, 2, PAD + S], at=m_at)
    PS = sb("PS", [P, 2, PAD + S], at=m_at + 8 * (PAD + S))
    PO = sb("PO", [P, 2, S], at=m_at + 16 * (PAD + S))
    PF = sb("PF", [P, 16], at=m_at + 24 * (PAD + S))

    QX = nc.dram_tensor("q_heads", (2, 16, HD, S), F32).ap()
    KX = nc.dram_tensor("k_heads", (2, 12, HD, S), F32).ap()
    VX = nc.dram_tensor("v_heads", (12, S, 2, HD), F32).ap()
    NF, NI = 14 * GRID, 9 * GRID
    BX = nc.dram_tensor("position_bias", (8, P, NF + NI), F32).ap()
    OH = sb("OH", [P, SLOTS, H], F32R, at=m_at)
    OL = sb("OL", [P, SLOTS, H], F32R, at=m_at + 4 * SLOTS * H)
    TA3 = sb("TA3", [P, 3, H], at=x_at + 20 * S)
    rope = sb("rope", [P, 2, S], at=acc_at)
    QN = sb("QN", [P, 2, H], at=x_at + 8 * S)
    RT = sb("RT", [P, 2, H], at=x_at + 12 * S)
    COS = sb("COS", [P, 2, H], at=t_at)
    RF = sb("RF", [P, 2, H], at=x_at + 16 * S)
    HR = sb("HR", [P, 2, 8])
    HX = sb("HX", [P, 4, P], at=t_at + 8 * S)
    VF = sb("VF", [P, NH, H], at=x_at + 26 * S)
    qg8 = sb("qg8", [P, 2])
    QS = sb("QS", [P, 2, S], F32R, at=m_at)
    KH = sb("KH", [P, 2, S], F32R, at=m_at + 8 * S)
    KL = sb("KL", [P, 2, S], F32R, at=m_at + 16 * S)
    VT = sb("VT", [P, 2, QT, P], F32R, at=m_at + 24 * S)
    bias = sb("bias", [P, 2, NF + NI], at=m_at + 32 * S)
    mask = sb("mask", [P, NF + NI], at=m_at + 32 * S + 8 * (NF + NI))
    SC = sb("biased", [P, 2, NI], at=t_at + 10 * S)
    PE_ = sb("probs", [P, 2, S], at=t_at)
    DG = sb("inverse_sums", [P, 2, P], at=t_at + 8 * S)
    neg_max = sb("neg_max", [P, 4])
    top_score = sb("top_score", [P, 2])
    den = sb("den", [P, 4])
    rden = sb("rden", [P, 4])
    PTh = sb("PTh", [P, 2, QT, H], F32R, at=h_at)
    PTl = sb("PTl", [P, 2, QT, H], F32R, at=h_at + 4 * KT * S)
    OT = sb("OT", [P, 2, H], at=acc_at)
    OS = sb("OS", [P, 2, H], at=acc_at + 8 * H)

    x_saved = nc.dram_tensor("x_saved", (D, S), F32).ap()

    PS_ALL = nc.alloc_psum_tensor("banks", [P, 8, H], F32)
    A, Dn, B6, B7 = PS_ALL[:, 0:2, :], PS_ALL[:, 2:6, :], PS_ALL[:, 6, :], PS_ALL[:, 7, :]
    SB_, TP, OB = PS_ALL[:, 0:4, :], PS_ALL[:, 4:6, :], PS_ALL[:, 6:8, :]

    def col(name):
        a, b = COLS[name]
        return cols[:, a:b]

    def con(name):
        a, b = CONST[name]
        return const[:, a:b]

    def half(hf):
        return slice(hf * H, (hf + 1) * H)

    def stats(hf):
        return (B6, A[:, 1, :])[hf]

    def pair_of(hf, v):
        return stats(hf)[:, 0:8].rearrange("p (t v) -> p v t", v=2)[:, v, :]

    def tile(order, i):
        return (i // KT, i % KT) if order == "down" else (i % 4 // 2, 2 * (i // 4) + i % 2)

    def sums(order, hf):
        return SUM if order == "down" or hf == 0 else SUM2

    def adds(order, i):
        return sum(1 <= tile(order, n)[1] < KT - 1 for n in range(i + 1))

    def complete(order, hf):
        return KT * (hf + 1) if order == "down" else 14 + 2 * hf

    def half_of(r):
        return r % 4 // 2 if r < 8 else r - 8

    sem = nc.alloc_semaphore
    cols_loaded, const_loaded, x_loaded = sem("cols_loaded"), sem("const_loaded"), sem("x_loaded")
    stage_in = [sem(f"stage_filled{i}") for i in range(STAGES)]
    unit_done = sem("unit_done")
    w_hi = sem("weight_hi")
    a_ready, a_free = sem("a_ready"), sem("a_free")
    d_ready, d_free = sem("d_ready"), sem("d_free")
    tb_ready = sem("tb_ready")
    ta_ready = sem("ta_ready")
    hi_done, lo_done = sem("hi_done"), sem("lo_done")
    sq_done, sum_done, stat_done = sem("square_done"), sem("sum_done"), sem("stat_done")
    g_sq_ready = sem("g_sq_ready")
    std_ready, both_ready, std1_ready = sem("std_ready"), sem("both_ready"), sem("std1_ready")
    x_rescaled = sem("x_rescaled")
    r1_own, r1_diag, r1_ready = sem("r1_own"), sem("r1_diag"), sem("r1_ready")
    rstd_own, diag_ready, rstd_ready = sem("rstd_own"), sem("diag_ready"), sem("rstd_ready")
    row_ready, row_copied = sem("row_ready"), sem("row_copied")
    pool_w_loaded, pool_w_split = sem("pool_w_loaded"), sem("pool_w_split")
    ada_half, ada_sum, mod_done = sem("ada_half"), sem("ada_sum"), sem("mod_done")
    dve_own, c_ready, set_ready = sem("dve_own"), sem("c_ready"), sem("set_ready")
    gain_ready = sem("gain_ready")
    ws_loaded, ws_masked, bs_ready = sem("ws_loaded"), sem("ws_masked"), sem("bs_ready")
    x_stored, x_back, x_back_first = sem("x_stored"), sem("x_back"), sem("x_back_first")
    bs_own, row_sum = sem("bs_own"), sem("row_sum")
    v_std, v_norm = sem("v_std"), sem("v_norm")
    mixed_own = sem("mixed_own")
    x_scaled = sem("x_scaled")
    slot_stored = [sem(f"slot_stored{i}") for i in range(SLOTS)]
    out_hi, out_lo = sem("slot_hi"), sem("slot_lo")
    rope_loaded, bias_built = sem("rope_loaded"), sem("bias_built")
    head_copied, ss_ready, sd_done = sem("head_copied"), sem("head_sums"), sem("head_std")
    hx_own, hx_done, hs_ready, cos_done = sem("hx_own"), sem("hx_done"), sem("hs_ready"), sem("cos_done")
    qn_done, rot_ready, rf_done = sem("head_normed"), sem("head_rotated"), sem("roped")
    qk_loaded = [sem(f"qk_loaded{i}") for i in range(2)]
    v_loaded = [sem(f"v_loaded{i}") for i in range(2)]
    bias_loaded = [sem(f"bias_loaded{i}") for i in range(2)]
    bias_masked, mask_loaded, bias_added = sem("bias_masked"), sem("mask_loaded"), sem("bias_added")
    s_ready, max_done, exp_done = sem("s_ready"), sem("max_done"), sem("exp_done")
    rd_own, rd_done = sem("rd_own"), sem("rd_done")
    t_ready, th_done, tl_done = sem("t_ready"), sem("th_done"), sem("tl_done")
    o_ready, ot_done, os_done, mixed_done = sem("o_ready"), sem("ot_done"), sem("os_done"), sem("mixed_done")
    po_ready, out_done = sem("pooled_ready"), sem("out_done")

    def src_in(w, c):
        return w.rearrange("(k p) n -> p k n", p=P)[:, :, bass.ds(c * UC, UC)]

    def src_w2(l, c):
        return w2[l].rearrange("(q p) n -> p q n", p=P)[:, bass.ds(c * FT, FT), :]

    def src_ada(l, cc, q):
        return ada_w[l].rearrange("(k p) n -> p k n", p=P)[:, 2 * q:2 * q + 2, bass.ds(cc * D, D)]

    src_pool = pool_w.rearrange("g (k p) n -> p (g k) n", p=P)

    def lagged(u, lag, kind, before):
        w = u - lag
        if w >= 0:
            return [(w, kind)]
        return [(w, before)] if before else []

    def banks(n):
        tiles = (n + P - 1) // P
        return [(0, 0, tiles // 2), (1, tiles // 2, tiles - tiles // 2)]

    def probs_t(x, u, k, m):
        return x[:, (u // 4) % 2, k:k + m, (u % 4) * P:(u % 4 + 1) * P]

    def width(kind, u):
        return S if kind == "A" else neighbourhood(u % QT)[1] * GRID

    def nothing(T, *_):
        pass

    def walk(eng, parts):
        do = {**dict.fromkeys(STEPS, nothing), **parts}
        T = Tally()

        def ada(l, cc, q):
            do["ada"](T, l, cc, q)
            T.add(u=1, ada=1)

        def mods(l, cc):
            do["mods"](T, l, cc)
            T.add(mod=1)

        def split(src):
            do["split"](T, src)
            T.add(u=1, w=1)
            T.n["uc"], T.n["un"] = T.n["un"], T.n["u"]

        def stores(kind, *args):
            n, dmas = {"heads": lambda what, j, nf: (2 * nf, 2 if what == "q" else 8), "plain": lambda *_: (4, 2),
                       "vals": lambda head, at, n: (QT, 4 if n == P else 2)}[kind](*args)
            for i in range(n):
                T.stored[(T.n["o"] + i) % SLOTS] += dmas

        def step(kind, nxt, counts, *args):
            if nxt is not None:
                split(nxt)
            else:
                T.n["uc"] = T.n["un"]
            do[kind](T, *args)
            if "o" in counts:
                stores(kind, *args)
            T.add(c=1, **counts)

        def norm(which, order="down"):
            do["norm"](T, which, order)
            count_norm(which == 4)
            T.add(b=16, h=16, g=1)

        A4 = dict(a=4, t=4, h=4)
        D16 = dict(d=16)

        def count_norm(dual=False):
            T.add(q=2 * KT, s=0 if dual else 12, st=2 * KT if dual else 4, n=2)

        do["start"](T)
        do["norm_pool"](T)
        T.add(u=24, mod=2, t=16, b=16, h=KT, g=1)
        count_norm()
        T.add(w=1)
        T.n["un"] = T.n["u"]
        step("pool", src_in(w1[0], 0), dict(d=16, mod=1), 1)

        def mlp(l, ada_passes):
            def up(par, nxt, first=False):
                step("up", nxt, A4, par, first)

            def down(par, nxt, ahead=4):
                step("down", nxt, D16, mod[:, l, 5 * KT:6 * KT], par, ahead)

            def passes(first, count, with_ada):
                def body(i):
                    for half_pass in range(2):
                        c = 2 * (i + first) + half_pass
                        if with_ada:
                            ada(1, i, 2 * half_pass)
                        up(1 - half_pass, src_w2(l, c))
                        if with_ada:
                            ada(1, i, 2 * half_pass + 1)
                        down(half_pass, src_in(w1[l], c + 2))
                    if with_ada:
                        mods(1, i)

                per = dict(u=4, uc=4, un=4, w=4, c=4, a=8, d=32, t=8, h=8)
                if with_ada:
                    per.update(u=8, uc=8, un=8, ada=4, mod=1)
                T.loop(eng, count, per, body)

            up(0, src_in(w1[l], 1), first=True)
            if ada_passes:
                passes(0, ada_passes, True)
            passes(ada_passes, CHUNKS // 2 - 1 - ada_passes, False)
            up(1, src_w2(l, CHUNKS - 2))
            down(0, src_w2(l, CHUNKS - 1))

        norm(1)
        mlp(0, 6)
        step("down", src_in(sgu_in, 4), D16, mod[:, 0, 5 * KT:6 * KT], 1, 0, 2)

        do["spill"](T)
        T.add(sp=1)
        norm(2)
        for j in range(4):
            step("values", src_in(sgu_in, (j + 5) % 8), dict(a=8), j)
            if j == 0:
                do["spatial"](T)
        def mix(j):
            do["mix"](T, j)
            T.add(d=4)

        for j in range(4):
            step("gates", src_in(sgu_in, j + 1) if j < 3 else src_in(sgu_out, 0), dict(a=4), j)
            if j == 0:
                do["normalise_v"](T)
            else:
                mix(j - 1)
            do["prepare"](T, j)
            T.add(h=4)
        mix(3)
        do["resplit"](T)
        T.add(h=2 * KT)
        for j in range(4):
            step("project", src_in(sgu_out, j + 1) if j < 3 else src_in(w1[1], 0), dict(d=4),
                 j, mod[:, 1, 2 * KT:3 * KT], j == 0, 3)
        norm(3, "project")
        do["rotation"](T)
        mlp(1, 0)
        step("down", src_in(w_in2, 0), D16, mod[:, 1, 5 * KT:6 * KT], 1, 0, 4)

        do["spill"](T)
        T.add(sp=1)
        norm(4)

        ahead = [src_in(w_in2, c) for c in range(1, 13)] + [src_in(w_out2, c) for c in range(4)] + [LOADED] * 2
        for T.lead in range(2):
            do["ahead"](T, ahead[T.lead])
        T.lead = 2

        def nxt(j):
            return ahead[j + T.lead]

        for j in range(2):
            step("heads", nxt(j), dict(a=4, o=4, ol=4, r=4), "q", j, FT)
        step("heads", nxt(2), dict(a=2, o=2, ol=2, r=2), "k", 0, 1)
        T.add(c=-1)
        do["v_a"](T)
        T.add(a=2)
        do["vals"](T, 0, P, P)
        stores("vals", 0, P, P)
        T.add(c=1, d=8, o=8, ol=8)
        for j in (3, 4):
            step("silu", nxt(j), dict(a=4), j - 3)
        for j in (5, 6):
            step("plain", nxt(j), dict(d=4, o=4, ol=4), "q", 8 + 4 * (j - 5))
        for j in (7, 8):
            step("plain", nxt(j), dict(d=4, o=4, ol=4), "k", 4 + 4 * (j - 7))
        for j in (9, 10):
            step("vals", nxt(j), dict(d=8, o=8, ol=8), 4 + 4 * (j - 9), 0, UC)
        for j in (11, 12):
            step("silu", nxt(j) if j < 12 else None, dict(a=4), 2 + j - 11)

        do["attend_start"](T)
        for kind in "AB":
            def pair(i, first=False, last=False, kind=kind):
                do["attend"](T, kind, i, ("A" if kind == "B" else None) if first else kind, last)
                T.add(v=PAIR, v2=2 * PAIR, vg=4)

            pair(0, first=True)
            T.loop(eng, 2, dict(v=PAIR, v2=2 * PAIR, vg=4), lambda i: pair(i + 1))
            pair(3, last=True)
        do["attend_end"](T)
        split(nxt(12))
        do["resplit"](T)
        T.add(h=2 * KT)
        for j in range(4):
            step("project", nxt(13 + j) if j < 3 else None, dict(d=4), j, ones[:, 0:KT], j == 0, 5)
        do["scale_x"](T)
        count_norm()
        T.add(x=2 * KT)
        do["finish"](T)

    def heads_of(kind, i, e):
        return (2 * i + e, i) if kind == "A" else (2 * i + e + 8, 2 * i + e + 4)

    def load_head(eng, T, kind, i, e, what, ahead=0):
        head, kv = heads_of(kind, i, e)
        if what == "v":
            reach(eng, o_ready, T("vg", 2 * e - 2 + 4 * ahead))
            eng.dma_start(VT[:, e].bitcast(F32), VX[bass.ds(kv, 1)]
                          .rearrange("a (k p) s d -> p (a k) (s d)", p=P)).then_inc(v_loaded[e], 16)
            return
        if what == "bias":
            eng.wait_ge(mask_loaded, 16)
            reach(eng, bias_added, T.b_units(QT * (e - 1) + PAIR * ahead))
            eng.dma_start(bias[:, e, :], BX[bass.ds(2 * i + e, 1)].rearrange("a p n -> p (a n)")) \
                .then_inc(bias_loaded[e], 16)
            return
        reach(eng, s_ready, T("v", QT * (e - 1) + PAIR * ahead))
        if T.n["v"] == 0 and not ahead:
            for s in range(SLOTS):
                eng.wait_ge(slot_stored[s], 16 * T.stored[s])
        buffer = {"q": QS, "kh": KH, "kl": KL}[what]
        if what == "q":
            src = QX[:, bass.ds(head, 1), :, :].rearrange("s h p n -> s (h p) n")
        else:
            src = KX["kh kl".split().index(what), bass.ds(kv, 1), :, :].broadcast_to([2, HD, S])
        for s in range(2):
            eng.dma_start(buffer[s * HD:(s + 1) * HD, e, :].bitcast(F32), src[s]).then_inc(qk_loaded[e], 16)

    def needed(kind):
        return ("q", "kh", "kl", "v") if kind == "A" else ("q", "kh", "kl", "v", "bias")

    block = nc.Block()
    with block:
        @block.sync
        def _(sync):
            def load(T, src):
                if src is LOADED:
                    return
                s = (T.n["u"] + T.lead) % STAGES
                reach(sync, unit_done, T("u", 1 - STAGES + T.lead))
                sync.dma_start(stage[:, s, :].rearrange("p (a n) -> p a n", a=src.shape[1]),
                               src).then_inc(stage_in[s], 16)

            def start(T):
                sync.dma_start(cols[:], cols_in).then_inc(cols_loaded, 16)

            def norm_pool(T):
                for u in range(24):
                    if u == 4:
                        for k in range(KT):
                            sync.dma_start(X[:, k, :], x_in[k * P:(k + 1) * P, :]).then_inc(x_loaded, 16)
                        sync.dma_start(const[:], const_in).then_inc(const_loaded, 16)
                    if u == 8:
                        sync.dma_start(PW[:].rearrange("p (a n) -> p a n", a=KT), src_pool).then_inc(pool_w_loaded, 16)
                    reach(sync, unit_done, u + 1 - STAGES)
                    sync.dma_start(stage[:, u % STAGES, :].rearrange("p (a n) -> p a n", a=2),
                                   src_ada(0, u // 4, u % 4)).then_inc(stage_in[u % STAGES], 16)

            def spill(T):
                if T("sp") == 1:
                    sync.wait_ge(x_back_first, 16 * FT)
                    sync.wait_ge(x_back, 16 * (KT - FT))
                for k in range(KT):
                    sync.wait_ge(d_free, T("d", KT + k + 1 - 16))
                    sync.dma_start(x_saved[k * P:(k + 1) * P, :], X[:, k, :]).then_inc(x_stored, 16)

            def spatial(T):
                sync.wait_ge(unit_done, T("u"))
                sync.wait_ge(mod_done, T("mod"))
                sync.dma_start(ws[:], sgu_ws.rearrange("h s t -> s h t")).then_inc(ws_loaded, 16)
                sync.dma_start(bs[:].rearrange("p h t -> p (h t)"),
                               bass.AP(sgu_bs.tensor, 0, [[0, P], [1, KT * P]])).then_inc(ws_loaded, 16)

            def resplit(T):
                sync.wait_ge(x_stored, 16 * KT * T("sp"))
                for k in range(KT):
                    sync.wait_ge(lo_done, T("h", KT + k + 1))
                    sync.dma_start(X[:, k, :], x_saved[k * P:(k + 1) * P, :]).then_inc(x_back_first if k < FT else x_back, 16)

            def store(T, i, n_dma, lo, pairs):
                sync.wait_ge(out_hi, T("o", i + 1))
                if lo is not None:
                    sync.wait_ge(out_lo, T("ol", lo + 1))
                for dst, src in pairs:
                    sync.dma_start(dst, src).then_inc(slot_stored[(T.n["o"] + i) % SLOTS], 16)

            def out_slot(T, i):
                s = (T.n["o"] + i) % SLOTS
                return OH[:, s, :].bitcast(F32), OL[:, s, :].bitcast(F32)

            def heads(T, what, j, nf):
                for i in range(2 * nf):
                    hf, f = i // nf, i % nf
                    hi, lo = out_slot(T, i)
                    if what == "q":
                        pairs = [(QX[s, 4 * j + 2 * f:4 * j + 2 * f + 2, :, half(hf)].rearrange("h p n -> (h p) n"), t)
                                 for s, t in enumerate((hi, lo))]
                    else:
                        pairs = [(KX[s, 2 * kv + r, :, half(hf)], t[HD * kv:HD * kv + HD])
                                 for s, t in enumerate((hi, lo)) for kv in range(2) for r in range(2)]
                    store(T, i, len(pairs), i, pairs)

            def plain(T, what, head):
                dst = QX if what == "q" else KX
                for i in range(4):
                    hf, f = i // 2, i % 2
                    hi, lo = out_slot(T, i)
                    store(T, i, 2, i, [(dst[s, head + 2 * f:head + 2 * f + 2, :, half(hf)].rearrange("h p n -> (h p) n"),
                                        t) for s, t in enumerate((hi, lo))])

            def vals(T, head, at, n):
                for i in range(QT):
                    hi, lo = out_slot(T, i)
                    tok = slice(i * P, (i + 1) * P)
                    pairs = []
                    for s, t in enumerate((hi, lo)):
                        t = t[:, 0:n].rearrange("p (h d) -> p h d", d=HD)
                        if n == P:
                            for r in range(2):
                                pairs.append((VX[r:4:2, tok, s, :].rearrange("h p d -> p h d"), t))
                        else:
                            pairs.append((VX[head:head + 4, tok, s, :].rearrange("h p d -> p h d"), t))
                    store(T, i, len(pairs), i, pairs)

            def attend_start(T):
                for e in range(2):
                    for what in ("q", "kh", "kl", "v"):
                        load_head(sync, T, "A", 0, e, what)
                sync.wait_ge(unit_done, T("u"))
                sync.wait_ge(a_ready, T("a"))
                sync.wait_ge(d_ready, T("d"))
                sync.wait_ge(bias_built, 16 * 32)
                sync.dma_start(mask[:], mask_in).then_inc(mask_loaded, 16)

            def position_bias(h):
                for par in range(2):
                    for row, n, at in ((1 - par, 14, 0), (3 - par, 9, NF)):
                        src = bass.AP(rpb.tensor, (h * 15 + row) * 127 + 63, [[127, n], [-1, GRID], [1, GRID]])
                        dst = BX[h, par * GRID:(par + 1) * GRID, at:at + n * GRID].rearrange("c (r k) -> r c k", k=GRID)
                        sync.dma_start(dst, src).then_inc(bias_built, 16)

            def values(T, j):
                position_bias(j)

            def gates(T, j):
                position_bias(4 + j)

            def rotation(T):
                sync.wait_ge(d_free, T("d"))
                sync.wait_ge(mod_done, T("mod"))
                sync.dma_start(rope[:], rope_in.rearrange("c p n -> p c n")).then_inc(rope_loaded, 16)

            def finish(T):
                sync.wait_ge(d_free, T("d"))
                for hf in range(NH):
                    for k in range(KT):
                        reach(sync, x_scaled, T("x", KT * hf + k + 1 - 16))
                        sync.dma_start(out[k * P:(k + 1) * P, half(hf)], X[:, k, half(hf)]).then_inc(out_done, 16)
                sync.wait_ge(out_done, 16 * KT * NH)

            walk(sync, dict(start=start, ahead=load, ada=lambda T, l, cc, q: load(T, src_ada(l, cc, q)),
                            split=load, norm_pool=norm_pool, spill=spill, values=values, gates=gates,
                            resplit=resplit, spatial=spatial, rotation=rotation, finish=finish,
                            heads=heads, vals=vals, plain=plain, attend_start=attend_start))

        @block.gpsimd
        def _(pool):
            def start(T):
                nc.gpsimd.memset(ones[:], 1.0).then_inc(set_ready, 1)
                nc.gpsimd.memset(epsc[:, 0:1], EPS).then_inc(set_ready, 1)
                nc.gpsimd.memset(epsc[:, 1:2], LN_EPS).then_inc(set_ready, 1)
                nc.gpsimd.memset(epsc[:, 2:3], EPS * EPS).then_inc(set_ready, 1)
                nc.gpsimd.memset(PH[:, :, 0:PAD], 0.0).then_inc(set_ready, 1)
                nc.gpsimd.memset(PS[:, :, 0:PAD], 0.0).then_inc(set_ready, 1)

            def add_squares(T, order, i):
                hf, k = tile(order, i)
                if not 1 <= k < KT - 1:
                    return
                acc_sum = sums(order, hf)
                pool.wait_ge(sq_done, T("q", i + 1))
                if k > 1:
                    last = max(n for n in range(i) if tile(order, n)[0] == hf)
                    pool.wait_ge(sum_done, T("s", adds(order, last)))
                else:
                    reach(pool, stat_done, T("st", 2 * hf if order == "down" else 0))
                first = SQ[:, (i - 1) % 2, :] if k == 1 else acc_sum[:]
                nc.gpsimd.tensor_tensor(acc_sum[:], first, SQ[:, i % 2, :], ALU.add).then_inc(sum_done, 1)

            def norm_pool(T):
                for i in range(2 * KT):
                    add_squares(T, "down", i)

            def down(T, gate, par, ahead, then=None):
                if then not in (None, 4):
                    for i in range(2 * KT):
                        add_squares(T, "down", i)

            def project(T, j, gate, first, then=None):
                for i in range(4 * j, 4 * j + 4):
                    add_squares(T, "project", i)

            def heads(T, what, j, nf):
                if T.n["r"] == 0:
                    pool.wait_ge(lo_done, T("h"))
                    pool.wait_ge(rope_loaded, 16)
                for i in range(2 * nf):
                    head_cos(T.n["r"] + i)

            def head_cos(r):
                pool.wait_ge(qn_done, r + 1)
                reach(pool, rf_done, r - 1)
                nc.gpsimd.tensor_tensor(COS[:, r % 2, :], QN[:, r % 2, :], rope[:, 0, half(half_of(r))],
                                        ALU.mult).then_inc(cos_done, 1)

            def spatial(T):
                pool.wait_ge(ws_loaded, 32)
                for h in range(KT):
                    nc.gpsimd.tensor_tensor(ws[:, h, :], ws[:, h, :], con("tri"), ALU.mult).then_inc(ws_masked, 1)

            def mask_bias(T, e):
                pool.wait_ge(mask_loaded, 16)
                pool.wait_ge(bias_loaded[e], T.loads(16, 4))
                nc.gpsimd.tensor_tensor(bias[:, e, :], bias[:, e, :], mask[:], ALU.add).then_inc(bias_masked, 1)

            def gated(T, g, tile):
                e = g // 2 % 2
                part, hf = slice(e * HD, (e + 1) * HD), g % 2
                reach(pool, mixed_done, T("vg", g))
                pool.wait_ge(os_done, T("vg", g + 1))
                dst = X[part, bass.ds(tile, 1), half(hf)].rearrange("p a n -> p (a n)")
                nc.gpsimd.tensor_tensor(dst, OS[part, g % 2, :], dst, ALU.mult).then_inc(mixed_done, 1)

            def attend(T, kind, i, before, last):
                for u in range(PAIR):
                    if kind == "B" and u in (0, 4):
                        reach(pool, mixed_done, T("vg", u // 4 - 2))
                        mask_bias(T, u // 4)
                    if kind == "B" and u in (3, 7):
                        pool.wait_ge(bias_masked, T.masked(u // 4))
                    for w, k in lagged(u, 8, kind, before):
                        if w % 4 == 3:
                            gated(T, w // 4, tile_of(kind, i, w < 0))

            def tile_of(kind, i, previous):
                return i + (4 if kind == "B" else 0) - (1 if previous else 0)

            def attend_end(T):
                gated(T, -2, KT - 1)
                gated(T, -1, KT - 1)

            walk(pool, dict(start=start, norm_pool=norm_pool,
                            pool=lambda T, then: down(T, None, None, None, then), down=down,
                            spatial=spatial, project=project, heads=heads, attend=attend,
                            attend_end=attend_end))

        @block.scalar
        def _(act):
            def start(T):
                act.wait_ge(cols_loaded, 16)
                nc.scalar.activation(c_act[:], col("c"), ACT.Silu).then_inc(c_ready, 1)

            def split(T, src):
                s = T.n["u"] % STAGES
                act.wait_ge(stage_in[s], T.fill() * 16)
                reach(act, a_ready, T("a"))
                reach(act, d_ready, T("d"))
                nc.scalar.activation(Whi[:, T.n["w"] % 2, :], stage[:, s, :], ACT.Copy).then_inc(w_hi, 1)

            def square(T, order, i, dual=False):
                hf, k = tile(order, i)
                if i < 2:
                    reach(act, stat_done, T("st"))
                    reach(act, sum_done, T("s"))
                elif dual:
                    act.wait_ge(stat_done, T("st", i - 1))
                else:
                    last_hf, last_k = tile(order, i - 2)
                    if last_k == KT - 1:
                        act.wait_ge(stat_done, T("st", 2 * last_hf + 2))
                    else:
                        act.wait_ge(sum_done, T("s", adds(order, i - 1 if last_k == 0 else i - 2)))
                nc.scalar.activation(SQ[:, i % 2, :], X[:, k, half(hf)], ACT.Square).then_inc(sq_done, 1)

            def deviation(T, order, hf, dual=False):
                act.wait_ge(set_ready, 6)
                act.wait_ge(stat_done, T("st", complete(order, hf) if dual else 2 * hf + 2))
                reach(act, rstd_own, T("n", hf))
                if dual:
                    nc.scalar.activation(std1[:, hf, :], pair_of(hf, 0), ACT.Sqrt, scale=1.0 / D,
                                         bias=epsc[:, 0:1]).then_inc(std1_ready, 1)
                    act.wait_ge(both_ready, hf + 1)
                source = both[:] if dual else stats(hf)[:, 0:4]
                nc.scalar.activation(std[:], source, ACT.Sqrt, scale=1.0 / D,
                                     bias=epsc[:, 2:3] if dual else epsc[:, 0:1]).then_inc(std_ready, 1)

            def norm_hi(T, which, n):
                hf, k = n // KT, n % KT
                shift = 0.0 if which == 4 else mod[:, which // 2, (which % 2) * 3 * KT + k:(which % 2) * 3 * KT + k + 1]
                act.wait_ge(tb_ready, T("b", n + 1))
                nc.scalar.activation(Hhi[:, k, half(hf)], NB[:, n % 4, :], ACT.Identity, bias=shift).then_inc(hi_done, 1)

            def completed(T, order, i, at, then):
                act.wait_ge(d_free, at)
                square(T, order, i, then == 4)
                if order == "down":
                    if i == 10:
                        deviation(T, order, 0, then == 4)
                    if i >= 14:
                        norm_hi(T, then, i - 14)

            def norm_pool(T):
                copy_row(0)
                act.wait_ge(x_loaded, 16 * KT)
                for i in range(2 * KT):
                    square(T, "down", i)
                    if i == 9:
                        deviation(T, "down", 0)
                copy_row(1)
                deviation(T, "down", 1)
                act.wait_ge(pool_w_loaded, 16)
                nc.scalar.activation(Whi[:, 0, :], PW[:], ACT.Copy).then_inc(w_hi, 1)
                act.wait_ge(gain_ready, T("g", 1))

                def pooled_hi(k):
                    act.wait_ge(po_ready, k + 1)
                    nc.scalar.activation(Hhi[:, k, :], PO[:, k % 2, :], ACT.Copy).then_inc(hi_done, 1)

                for k in range(KT):
                    if k >= 2:
                        act.wait_ge(po_ready, k - 1)
                    for hf in range(NH):
                        act.wait_ge(tb_ready, T("b", KT * hf + k + 1))
                        nc.scalar.activation(PH[:, k % 2, PAD + hf * H:PAD + (hf + 1) * H], XN[:, k, half(hf)],
                                             ACT.Identity, scale=gain[:, 0, k:k + 1],
                                             bias=mod[:, 0, k:k + 1]).then_inc(ta_ready, 1)
                    if k >= 1:
                        pooled_hi(k - 1)
                    if k in (1, 3, 6):
                        copy_row({1: 2, 3: 3, 6: 4}[k])
                pooled_hi(KT - 1)
                copy_row(5)

            def copy_row(cc):
                act.wait_ge(row_ready, cc + 1)
                act.wait_ge(unit_done, 4 * cc + 4)
                if cc == 4:
                    act.wait_ge(pool_w_split, 1)
                for h in range(2):
                    nc.scalar.activation(rows[cc // 2][0:1, cc % 2, half(h)],
                                         Dn[0:1, 2 * (cc % 2) + h, :], ACT.Copy).then_inc(row_copied, 1)

            def norm(T, which, order):
                if order == "project":
                    deviation(T, order, 0)
                else:
                    norm_hi(T, which, 2)
                deviation(T, order, 1, which == 4)
                for n in range(3 if order == "down" else 0, 2 * KT):
                    norm_hi(T, which, n)

            def down(T, gate, par, ahead, then=None):
                if then is not None:
                    for i in range(2 * KT):
                        completed(T, "down", i, T("d", i + 1), then)

            def pool(T, then):
                down(T, None, None, None, then)

            def project(T, j, gate, first, then=None):
                if then is not None:
                    for i in range(4):
                        completed(T, "project", 4 * j + i, T("d", i + 1), then)

            def up(T, par, first):
                for hf in range(NH):
                    for f in range(FT):
                        i = hf * FT + f
                        act.wait_ge(a_ready, T("a", i + 1))
                        if first and i == 0:
                            act.wait_ge(lo_done, T("h"))
                        act.wait_ge(ta_ready, T("t", i - 1))
                        nc.scalar.activation(TB[:, i % 2, :], A[:, i % 2, :], ACT.Relu).then_inc(a_free, 1)
                        act.wait_ge(a_free, T("a", i + 1))
                        act.wait_ge(lo_done, T("h", i - 1))
                        nc.scalar.activation(TA[:, i % 2, :], TB[:, i % 2, :], ACT.Square).then_inc(ta_ready, 1)
                        act.wait_ge(ta_ready, T("t", i + 1))
                        nc.scalar.activation(Mhi[:, par, f, half(hf)], TA[:, i % 2, :], ACT.Copy).then_inc(hi_done, 1)

            def values(T, j):
                for i in range(KT):
                    act.wait_ge(a_ready, T("a", i + 1))
                    nc.scalar.activation(V[:, i, j * UC:(j + 1) * UC], A[:, i % 2, 0:UC], ACT.Gelu).then_inc(a_free, 1)

            def gates(T, j):
                for hf in range(NH):
                    for f in range(FT):
                        i = hf * FT + f
                        act.wait_ge(a_ready, T("a", i + 1))
                        act.wait_ge(x_stored, 16 * KT * T("sp"))
                        nc.scalar.activation(X[:, j * FT + f, half(hf)], A[:, i % 2, :], ACT.Gelu).then_inc(a_free, 1)

            def normalise_v(T):
                act.wait_ge(v_norm, 1)
                nc.scalar.activation(vstd[:], mv[:, :, 1], ACT.Sqrt, scale=1.0, bias=epsc[:, 1:2]).then_inc(v_std, 1)

            def prepare(T, j):
                act.wait_ge(v_norm, 2)
                act.wait_ge(ws_masked, KT)
                act.wait_ge(row_sum, 1)
                reach(act, d_ready, T("d"))
                for h in range(2):
                    nc.scalar.activation(WShi[:, h, :], ws[:, 2 * j + h, :], ACT.Copy).then_inc(hi_done, 1)
                    nc.scalar.activation(Vhi[:, h], V[:, :, (2 * j + h) * P:(2 * j + h + 1) * P],
                                         ACT.Copy).then_inc(hi_done, 1)

            def resplit(T):
                if T("v") > 0:
                    act.wait_ge(mixed_done, T("vg"))
                act.wait_ge(d_free, T("d"))
                act.wait_ge(a_ready, T("a"))
                for hf in range(NH):
                    for k in range(KT):
                        nc.scalar.activation(Hhi[:, k, half(hf)], X[:, k, half(hf)], ACT.Copy).then_inc(hi_done, 1)

            def scale_x(T):
                for hf in range(NH):
                    deviation(T, "project", hf)

            def slot_for(T, i):
                slot = (T.n["o"] + i) % SLOTS
                stored = T.stored[slot] - (2 if i < 0 else 0)
                reach(act, slot_stored[slot], 16 * stored)
                return slot

            def heads(T, what, j, nf):
                for i in range(2 * nf):
                    r = T.n["r"] + i
                    act.wait_ge(a_ready, T("a", i + 1))
                    reach(act, qn_done, r - 2)
                    reach(act, ss_ready, r - 1)
                    if r < 2:
                        act.wait_ge(lo_done, T("h"))
                        act.wait_ge(x_stored, 16 * KT * T("sp"))
                    nc.scalar.activation(TA3[:, r % 3, :], A[:, i % 2, :], ACT.Copy).then_inc(head_copied, 1)
                    nc.scalar.activation(TB[:, r % 2, :], A[:, i % 2, :], ACT.Square).then_inc(a_free, 1)
                    head_std(r - 1)
                    head_hi(T, r - 3, i - 3)
                if what == "k":
                    head_std(r)
                    for back in (2, 1, 0):
                        head_hi(T, r - back, i - back)

            def head_std(r):
                if r >= 0:
                    act.wait_ge(ss_ready, r + 1)
                    reach(act, hx_own, r - 1)
                    nc.scalar.activation(HR[:, r % 2, :], Dn[:, 0, 0:8], ACT.Sqrt, scale=1.0 / HD,
                                         bias=epsc[:, 0:1]).then_inc(sd_done, 1)

            def head_hi(T, r, i):
                if r >= 0:
                    act.wait_ge(rf_done, r + 1)
                    nc.scalar.activation(OH[:, slot_for(T, i), :], RF[:, r % 2, :], ACT.Copy).then_inc(out_hi, 1)

            def plain(T, what, head):
                for i in range(4):
                    slot = slot_for(T, i)
                    act.wait_ge(d_ready, T("d", i + 1))
                    nc.scalar.activation(OH[:, slot, :], Dn[:, i, :], ACT.Copy,
                                         scale=HD ** -0.5 if what == "q" else 1.0).then_inc(out_hi, 1)

            def v_a(T):
                for hf in range(NH):
                    act.wait_ge(a_ready, T("a", hf + 1))
                    nc.scalar.activation(VF[:, hf, :], A[:, hf, :], ACT.Copy).then_inc(a_free, 1)

            def vals(T, head, at, n):
                for i in range(QT):
                    slot = slot_for(T, i)
                    act.wait_ge(d_ready, T("d", i + 1))
                    nc.scalar.activation(OH[:, slot, 0:n], Dn[:, i % 4, 0:n], ACT.Copy).then_inc(out_hi, 1)

            def silu(T, j):
                for i in range(4):
                    hf, f = i // 2, i % 2
                    act.wait_ge(a_ready, T("a", i + 1))
                    act.wait_ge(out_lo, T.n["r"])
                    nc.scalar.activation(X[:, j * FT + f, half(hf)], A[:, i % 2, :], ACT.Silu).then_inc(a_free, 1)

            def exp(T, u, kind, n):
                act.wait_ge(max_done, T("v", u + 1))
                reach(act, t_ready, T("v2", 2 * u - 2))
                scores = SB_[:, 2 * (u % 2):2 * (u % 2) + 2, :].rearrange("p b n -> p (b n)")[:, 0:n]
                if kind == "B":
                    scores = SC[:, u % 2, 0:n]
                nc.scalar.activation(PE_[:, u % 2, 0:n], scores, ACT.Exp, bias=neg_max[:, u % 4:u % 4 + 1],
                                     accum_out=den[:, u % 4:u % 4 + 1]).then_inc(exp_done, 1)

            def probs_hi(T, u, n):
                for g, first, m in banks(n):
                    act.wait_ge(t_ready, T("v2", 2 * u + g + 1))
                    if u % 4 == 0:
                        reach(act, o_ready, T("vg", u // 4 - 1))
                    nc.scalar.activation(probs_t(PTh, u, first, m), TP[:, g, 0:m * P]
                                         .rearrange("p (k q) -> p k q", q=P), ACT.Copy).then_inc(th_done, 1)

            def lower_half(T, g):
                act.wait_ge(o_ready, T("vg", g + 1))
                reach(act, os_done, T("vg", g - 1))
                nc.scalar.activation(OT[0:HD, g % 2, :], OB[HD:P, g % 2, :], ACT.Copy).then_inc(ot_done, 1)

            def attend(T, kind, i, before, last):
                following = ("B", 0) if last else (kind, i + 1)
                for u in range(PAIR):
                    for w, k in lagged(u, 3, kind, before):
                        probs_hi(T, w, width(k, w))
                    if before is not None and u in LOAD_AT and LOAD_AT[u] in needed(kind):
                        load_head(nc.scalar, T, kind, i, 1, LOAD_AT[u])
                    if u - QT in LOAD_AT and not (last and kind == "B") and LOAD_AT[u - QT] in needed(following[0]):
                        load_head(nc.scalar, T, *following, 0, LOAD_AT[u - QT], ahead=1)
                    for w, k in lagged(u, 1, kind, before):
                        exp(T, w, k, width(k, w))
                    for w, k in lagged(u, 8, kind, before):
                        if w % 4 == 3:
                            lower_half(T, w // 4)

            def attend_end(T):
                probs_hi(T, -3, width("B", -3))
                exp(T, -1, "B", width("B", -1))
                for u in (-2, -1):
                    probs_hi(T, u, width("B", u))
                lower_half(T, -2)
                lower_half(T, -1)

            walk(act, dict(start=start, prepare=prepare, v_a=v_a, split=split, norm_pool=norm_pool,
                           norm=norm, pool=pool, up=up, down=down, values=values, gates=gates,
                           normalise_v=normalise_v, resplit=resplit, project=project, scale_x=scale_x, heads=heads,
                           vals=vals, silu=silu, plain=plain, attend=attend, attend_end=attend_end))

        @block.vector
        def _(dve):
            own = [0]

            def chained(instruction):
                own[0] += 1
                instruction.then_inc(dve_own, 1)
                dve.wait_ge(dve_own, own[0])

            def start(T):
                dve.wait_ge(c_ready, 1)

            def ada(T, l, cc, q):
                s = T.n["u"] % STAGES
                if q == 0:
                    reach(dve, ada_sum, T("mod"))
                dve.wait_ge(stage_in[s], T.fill() * 16)
                reach(dve, unit_done, T("u"))
                if q == 0:
                    nc.vector.tensor_scalar(out=acc[:], in0=stage[:, s, 0:D], scalar1=c_act[:, 0:1], scalar2=None,
                                            op0=ALU.mult).then_inc(ada_half, 1)
                else:
                    nc.vector.scalar_tensor_tensor(out=acc[:], in0=stage[:, s, 0:D], scalar=c_act[:, 2 * q:2 * q + 1],
                                                   in1=acc[:], op0=ALU.mult, op1=ALU.add).then_inc(ada_half, 1)
                dve.wait_ge(ada_half, T("ada", 1))
                nc.vector.scalar_tensor_tensor(out=acc[:], in0=stage[:, s, D:2 * D],
                                               scalar=c_act[:, 2 * q + 1:2 * q + 2], in1=acc[:], op0=ALU.mult,
                                               op1=ALU.add).then_inc(unit_done, 1)

            def mods(T, l, cc):
                dve.wait_ge(ada_sum, T("mod", 1))
                b = COLS[f"ada_b{l}"][0]
                nc.vector.tensor_tensor(mod[:, l, bass.ds(cc * KT, KT)], B6[:, 0:KT],
                                        cols[:, bass.ds(cc * KT + b, KT)], ALU.add).then_inc(mod_done, 1)

            def split(T, src):
                s, w = T.n["u"] % STAGES, T.n["w"] % 2
                dve.wait_ge(w_hi, T("w", 1))
                nc.vector.tensor_tensor(Wlo[:, w, :], stage[:, s, :], Whi[:, w, :].bitcast(F32),
                                        ALU.subtract).then_inc(unit_done, 1)

            def make_gain(T, which):
                if which == 4:
                    nc.vector.tensor_scalar(out=g_sq[:, :, 0], in0=col("final_g"), scalar1=0.0, scalar2=1.0,
                                            op0=ALU.mult, op1=ALU.add).then_inc(g_sq_ready, 1)
                    nc.vector.tensor_tensor(g_sq[:, :, 1], col("final_g"), col("final_g"),
                                            ALU.mult).then_inc(g_sq_ready, 1)
                    nc.vector.tensor_tensor(gain[:, 4, :], col("final_g"), col("gain2"), ALU.mult).then_inc(gain_ready, 1)
                    return
                l, sc = which // 2, (which % 2) * 3 * KT + KT
                dve.wait_ge(mod_done, T("mod"))
                nc.vector.scalar_tensor_tensor(out=gain[:, which, :], in0=mod[:, l, sc:sc + KT], scalar=1.0,
                                               in1=col(("mix_g", "mlp_g")[which % 2] + str(l)), op0=ALU.add,
                                               op1=ALU.mult).then_inc(gain_ready, 1)

            def invert(T, hf, dual=False):
                if dual:
                    dve.wait_ge(stat_done, T("st", complete("down", hf)))
                    reach(dve, std_ready, T("n", hf))
                    dve.wait_ge(std1_ready, hf + 1)
                    nc.vector.tensor_scalar(out=both[:], in0=pair_of(hf, 0), scalar1=EPS, scalar2=None,
                                            op0=ALU.mult).then_inc(dve_own, 1)
                    own[0] += 1
                    dve.wait_ge(dve_own, own[0])
                    nc.vector.tensor_tensor(both[:], both[:], pair_of(hf, 1), ALU.add) \
                        .then_inc(both_ready, 1)
                dve.wait_ge(std_ready, T("n", hf + 1))
                reach(dve, diag_ready, T("n", hf))
                nc.vector.reciprocal(rstd[:], std[:]).then_inc(rstd_own, 1)
                dve.wait_ge(rstd_own, T("n", hf + 1))
                reach(dve, rstd_ready, T("n", hf))
                if T.n["n"] == 0:
                    dve.wait_ge(const_loaded, 16)
                for t in range(4):
                    ins = nc.vector.tensor_scalar(out=diag[:, t * P:(t + 1) * P], in0=con("ident"),
                                                  scalar1=rstd[:, t:t + 1], scalar2=None, op0=ALU.mult)
                ins.then_inc(diag_ready, 1)

            def norm_pool(T):
                for hf, bank in enumerate((B7, B6)):
                    invert(T, hf)
                    dve.wait_ge(rstd_ready, T("n", hf + 1))
                    for k in range(KT):
                        nc.vector.tensor_tensor(XN[:, k, half(hf)], X[:, k, half(hf)], bank,
                                                ALU.mult).then_inc(tb_ready, 1)
                dve.wait_ge(pool_w_loaded, 16)
                dve.wait_ge(w_hi, 1)
                nc.vector.tensor_tensor(Wlo[:, 0, :], PW[:], Whi[:, 0, :].bitcast(F32),
                                        ALU.subtract).then_inc(pool_w_split, 1)
                mods0(T, 0)
                T.add(mod=1)
                make_gain(T, 0)
                dve.wait_ge(set_ready, 6)
                for k in range(KT):
                    dve.wait_ge(ta_ready, T("t", 2 * k + 2))
                    group, last, reach_back = k // 2, PH[:, k % 2, :], 1
                    for j in range(group + 1):
                        chained(nc.vector.tensor_tensor(PS[:, j % 2, PAD:], last[:, PAD:],
                                                        last[:, PAD - reach_back:PAD + S - reach_back], ALU.add))
                        last, reach_back = PS[:, j % 2, :], 2 * reach_back
                    if k >= 2:
                        dve.wait_ge(hi_done, T("h", k - 1))
                        dve.wait_ge(lo_done, T("h", k - 1))
                    chained(nc.vector.scalar_tensor_tensor(out=PO[:, k % 2, :], in0=last[:, PAD:],
                                                           scalar=1.0 / WINDOWS[group], in1=PH[:, k % 2, PAD:],
                                                           op0=ALU.mult, op1=ALU.subtract))
                    chained(nc.vector.tensor_tensor(PF[:], last[:, PAD:PAD + 16],
                                                    con("invc")[:, group * 16:(group + 1) * 16], ALU.mult))
                    nc.vector.tensor_tensor(PO[:, k % 2, 0:16], PF[:], PH[:, k % 2, PAD:PAD + 16],
                                            ALU.subtract).then_inc(po_ready, 1)
                    if k >= 1:
                        pooled_lo(T, k - 1)
                pooled_lo(T, KT - 1)
                mods0(T, 1)
                T.add(mod=-1)

            def mods0(T, pair):
                dve.wait_ge(ada_sum, T("mod", 1))
                at = slice(2 * KT * pair, 2 * KT * (pair + 1))
                nc.vector.tensor_tensor(mod[:, 0, at], A[:, 0, at], col("ada_b0")[:, at], ALU.add).then_inc(mod_done, 1)

            def pooled_lo(T, k):
                dve.wait_ge(hi_done, T("h", k + 1))
                nc.vector.tensor_tensor(Hlo[:, k, :], PO[:, k % 2, :], Hhi[:, k, :].bitcast(F32),
                                        ALU.subtract).then_inc(lo_done, 1)

            def split_lo(T, i, out_lo, out_hi):
                dve.wait_ge(hi_done, T("h", i + 1))
                nc.vector.tensor_tensor(out_lo, TA[:, i % 2, :], out_hi.bitcast(F32),
                                        ALU.subtract).then_inc(lo_done, 1)

            def norm_scaled(T, which, n):
                hf, k = n // KT, n % KT
                if k == 0:
                    dve.wait_ge(rstd_ready, T("n", hf + 1))
                dve.wait_ge(gain_ready, T("g", 1))
                reach(dve, lo_done, T("h", n - 3))
                nc.vector.scalar_tensor_tensor(out=NB[:, n % 4, :], in0=X[:, k, half(hf)],
                                               scalar=gain[:, which, k:k + 1], in1=(B7, Dn[:, 0, :])[hf],
                                               op0=ALU.mult, op1=ALU.mult).then_inc(tb_ready, 1)

            def norm_lo(T, which, n):
                hf, k = n // KT, n % KT
                shift = 0.0 if which == 4 else mod[:, which // 2, (which % 2) * 3 * KT + k:(which % 2) * 3 * KT + k + 1]
                dve.wait_ge(hi_done, T("h", n + 1))
                nc.vector.scalar_tensor_tensor(out=Hlo[:, k, half(hf)], in0=NB[:, n % 4, :], scalar=shift,
                                               in1=Hhi[:, k, half(hf)].bitcast(F32), op0=ALU.add,
                                               op1=ALU.subtract).then_inc(lo_done, 1)

            def completed(T, i, then):
                if i == 0 and then != 1:
                    make_gain(T, then)
                if i == 7 and then == 1:
                    mods0(T, 2)
                    T.add(mod=1)
                    make_gain(T, then)
                    T.add(mod=-1)
                if i == 11:
                    invert(T, 0, then == 4)
                if i >= 13:
                    norm_scaled(T, then, i - 13)
                if i >= 15:
                    norm_lo(T, then, i - 15)

            def norm(T, which, order):
                begun = 3 if order == "down" else 0
                if not begun:
                    make_gain(T, which)
                    invert(T, 0)
                for n in range(begun, 2 * KT + 2):
                    if n == begun + 2:
                        invert(T, 1, which == 4)
                    if n < 2 * KT:
                        norm_scaled(T, which, n)
                    if n >= 2:
                        norm_lo(T, which, n - 2)

            def up(T, par, first):
                for hf in range(NH):
                    for f in range(FT):
                        split_lo(T, hf * FT + f, Mlo[:, par, f, half(hf)], Mhi[:, par, f, half(hf)])

            def add_to_x(T, gate, then):
                for hf in range(NH):
                    for k in range(KT):
                        i = hf * KT + k
                        dve.wait_ge(d_ready, T("d", i + 1))
                        reach(dve, d_free, T("d", i - 15))
                        nc.vector.scalar_tensor_tensor(out=X[:, k, half(hf)], in0=Dn[:, i % D_BANKS, :],
                                                       scalar=gate[:, k:k + 1], in1=X[:, k, half(hf)],
                                                       op0=ALU.mult, op1=ALU.add).then_inc(d_free, 1)
                        if then is not None:
                            completed(T, i, then)

            def pool(T, then):
                dve.wait_ge(mod_done, T("mod"))
                chained(nc.vector.tensor_tensor(pg[:], mod[:, 0, 2 * KT:3 * KT], col("pool_scale"), ALU.mult))
                add_to_x(T, pg, then)

            def down(T, gate, par, ahead, then=None):
                add_to_x(T, gate, then)

            def spatial(T):
                dve.wait_ge(ws_loaded, 32)
                dve.wait_ge(row_sum, 1)
                for h in range(KT):
                    bank = (B6, B7)[h // 4]
                    nc.vector.scalar_tensor_tensor(out=bs[:, h, :], in0=bank[:, h % 4 * P:(h % 4 + 1) * P],
                                                   scalar=col("ln_b")[:, h:h + 1], in1=bs[:, h, :],
                                                   op0=ALU.mult, op1=ALU.add).then_inc(bs_ready, 1)

            def normalise_v(T):
                dve.wait_ge(a_free, T("a", -4))
                for i in range(KT):
                    for b in range(2):
                        nc.vector.bn_stats(bstat[:, i, b, :], V[:, i, b * H:(b + 1) * H]).then_inc(bs_own, 1)
                for i in range(KT):
                    dve.wait_ge(bs_own, 2 * i + 2)
                    ins = nc.vector.bn_aggr(mv[:, i, :], bstat[:, i].rearrange("p b s -> p (b s)"))
                ins.then_inc(v_norm, 1)
                dve.wait_ge(v_std, 1)
                chained(nc.vector.reciprocal(vrs[:], vstd[:]))
                for i in range(KT):
                    ins = nc.vector.tensor_scalar(out=V[:, i, :], in0=V[:, i, :], scalar1=mv[:, i, 0:1],
                                                  scalar2=vrs[:, i:i + 1], op0=ALU.subtract, op1=ALU.mult)
                ins.then_inc(v_norm, 1)

            def prepare(T, j):
                for h in range(2):
                    dve.wait_ge(hi_done, T("h", 2 * h + 1))
                    nc.vector.tensor_tensor(WSlo[:, h, :], ws[:, 2 * j + h, :], WShi[:, h, :].bitcast(F32),
                                            ALU.subtract).then_inc(lo_done, 1)
                    dve.wait_ge(hi_done, T("h", 2 * h + 2))
                    nc.vector.tensor_tensor(Vlo[:, h], V[:, :, (2 * j + h) * P:(2 * j + h + 1) * P],
                                            Vhi[:, h].bitcast(F32), ALU.subtract).then_inc(lo_done, 1)

            def mix(T, j):
                for h in range(2):
                    head = 2 * j + h
                    for hf in range(NH):
                        i = 2 * h + hf
                        dve.wait_ge(d_ready, T("d", i + 1))
                        dve.wait_ge(a_free, T("a"))
                        dve.wait_ge(bs_ready, KT)
                        bank = Dn[:, i % D_BANKS, :]
                        chained(nc.vector.scalar_tensor_tensor(
                            out=bank.rearrange("p (n t) -> p n t", t=P), in0=bank.rearrange("p (n t) -> p n t", t=P),
                            scalar=col("ln_g")[:, head:head + 1],
                            in1=bs[:, head:head + 1, :].broadcast_to([P, 4, P]), op0=ALU.mult, op1=ALU.add))
                        nc.vector.tensor_tensor(X[:, head, half(hf)], bank, X[:, head, half(hf)],
                                                ALU.mult).then_inc(d_free, 1)

            def resplit(T):
                for hf in range(NH):
                    if T("sp") == 2:
                        first_rstd(T, hf)
                    for k in range(KT):
                        dve.wait_ge(hi_done, T("h", hf * KT + k + 1))
                        nc.vector.tensor_tensor(Hlo[:, k, half(hf)], X[:, k, half(hf)],
                                                Hhi[:, k, half(hf)].bitcast(F32), ALU.subtract).then_inc(lo_done, 1)

            def first_rstd(T, hf):
                reach(dve, r1_diag, hf)
                nc.vector.reciprocal(rstd[:], std1[:, hf, :]).then_inc(r1_own, 1)
                dve.wait_ge(r1_own, hf + 1)
                reach(dve, r1_ready, hf)
                for t in range(4):
                    ins = nc.vector.tensor_scalar(out=diag[:, t * P:(t + 1) * P], in0=con("ident"),
                                                  scalar1=rstd[:, t:t + 1], scalar2=None, op0=ALU.mult)
                ins.then_inc(r1_diag, 1)

            def rescale(T, j):
                for i in range(4):
                    hf, k = i // 2, FT * j + i % 2
                    dve.wait_ge(r1_ready, hf + 1)
                    nc.vector.scalar_tensor_tensor(out=X[:, k, half(hf)], in0=X[:, k, half(hf)],
                                                   scalar=col("final_g")[:, k:k + 1], in1=A[:, hf, :],
                                                   op0=ALU.mult, op1=ALU.mult).then_inc(x_rescaled, 1)

            def project(T, j, gate, first, then=None):
                if j == 0:
                    dve.wait_ge(x_back_first, 16 * FT * T("sp"))
                if j == 1:
                    dve.wait_ge(x_back, 16 * (KT - FT) * T("sp"))
                if then == 5:
                    rescale(T, j)
                    dve.wait_ge(x_rescaled, 4 * j + 4)
                for i in range(4):
                    hf, k = i // 2, FT * j + i % 2
                    dve.wait_ge(d_ready, T("d", i + 1))
                    nc.vector.scalar_tensor_tensor(out=X[:, k, half(hf)], in0=Dn[:, i, :], scalar=gate[:, k:k + 1],
                                                   in1=X[:, k, half(hf)], op0=ALU.mult, op1=ALU.add).then_inc(d_free, 1)

            def heads(T, what, j, nf):
                if T.n["r"] == 0:
                    chained(nc.vector.tensor_scalar(out=qg8[:, 0:1], in0=col("qg"), scalar1=HD ** -0.5, scalar2=None,
                                                    op0=ALU.mult))
                    dve.wait_ge(rope_loaded, 16)
                for i in range(2 * nf):
                    r = T.n["r"] + i
                    head_invert(r - 1)
                    head_norm(r - 2)
                    head_rope(T, r - 3, half_of(r - 3), i - 3)
                if what == "k":
                    head_invert(r)
                    head_norm(r - 1)
                    head_rope(T, r - 2, half_of(r - 2), i - 2)
                    head_norm(r)
                    head_rope(T, r - 1, half_of(r - 1), i - 1)
                    head_rope(T, r, half_of(r), i)

            def head_invert(r):
                if r >= 0:
                    dve.wait_ge(sd_done, r + 1)
                    nc.vector.reciprocal(HR[:, r % 2, :], HR[:, r % 2, :]).then_inc(hx_own, 1)
                    dve.wait_ge(hx_own, r + 1)
                    reach(dve, hs_ready, r)
                    nc.vector.tensor_copy(HX[:].rearrange("p t (h d) -> p (t h) d", d=HD),
                                          HR[:, r % 2, :].unsqueeze(2).broadcast_to([P, 8, HD])).then_inc(hx_done, 1)

            def head_norm(r):
                if r >= 0:
                    g = qg8[:, 0:1] if r < 8 else col("kg")
                    dve.wait_ge(hs_ready, r + 1)
                    dve.wait_ge(head_copied, r + 1)
                    reach(dve, rot_ready, r - 1)
                    reach(dve, cos_done, r - 1)
                    nc.vector.scalar_tensor_tensor(out=QN[:, r % 2, :], in0=TA3[:, r % 3, :], scalar=g,
                                                   in1=B6, op0=ALU.mult, op1=ALU.mult).then_inc(qn_done, 1)

            def head_rope(T, r, hf, i):
                if r >= 0:
                    dve.wait_ge(rot_ready, r + 1)
                    chained(nc.vector.tensor_tensor(RT[:, 1, :], B7, rope[:, 1, half(hf)], ALU.mult))
                    dve.wait_ge(cos_done, r + 1)
                    reach(dve, out_hi, r - 1)
                    nc.vector.tensor_tensor(RF[:, r % 2, :], COS[:, r % 2, :], RT[:, 1, :], ALU.add).then_inc(rf_done, 1)
                    slot = (T.n["o"] + i) % SLOTS
                    dve.wait_ge(out_hi, T("o", i + 1))
                    nc.vector.tensor_tensor(OL[:, slot, :], RF[:, r % 2, :], OH[:, slot, :].bitcast(F32),
                                            ALU.subtract).then_inc(out_lo, 1)

            def plain(T, what, head):
                for i in range(4):
                    slot = (T.n["o"] + i) % SLOTS
                    dve.wait_ge(out_hi, T("o", i + 1))
                    nc.vector.scalar_tensor_tensor(out=OL[:, slot, :], in0=Dn[:, i, :],
                                                   scalar=HD ** -0.5 if what == "q" else 1.0,
                                                   in1=OH[:, slot, :].bitcast(F32), op0=ALU.mult,
                                                   op1=ALU.subtract).then_inc(d_free, 1)
                    out_lo_too(T, i, slot)

            def out_lo_too(T, i, slot):
                dve.wait_ge(d_free, T("d", i + 1))
                nc.vector.tensor_copy(OL[:, slot, 0:1], OL[:, slot, 0:1].bitcast(F32)).then_inc(out_lo, 1)

            def vals(T, head, at, n):
                for i in range(QT):
                    slot = (T.n["o"] + i) % SLOTS
                    dve.wait_ge(out_hi, T("o", i + 1))
                    nc.vector.tensor_tensor(OL[:, slot, 0:n], Dn[:, i % 4, 0:n], OH[:, slot, 0:n].bitcast(F32),
                                            ALU.subtract).then_inc(d_free, 1)
                    out_lo_too(T, i, slot)

            def row_maxima(T, u, kind, n):
                at = u % 4
                if kind == "A":
                    dve.wait_ge(s_ready, T("v", u + 1))
                    scores = SB_[:, 2 * (u % 2):2 * (u % 2) + 2, :].rearrange("p b n -> p (b n)")[:, 0:n]
                else:
                    first, rows = neighbourhood(u % QT)
                    b0 = (first - 2 * (u % QT) + 6) * GRID if rows == NKH else NF
                    if u % QT == 0:
                        dve.wait_ge(bias_masked, T.masked(u // QT))
                    dve.wait_ge(s_ready, T("v", u + 1))
                    reach(dve, exp_done, T("v", u - 1))
                    scores = SC[:, u % 2, 0:n]
                    bank = SB_[:, 2 * (u % 2):2 * (u % 2) + 2, :].rearrange("p b n -> p (b n)")[:, 0:n]
                    nc.vector.memset(top_score[:, 1:2], 0.0)
                    nc.vector.tensor_tensor_reduce(out=scores, in0=bank, in1=bias[:, u // QT % 2, b0:b0 + n], scale=1.0,
                                                   scalar=-3e38, op0=ALU.add, op1=ALU.max,
                                                   accum_out=top_score[:, 0:1]).then_inc(bias_added, 1)
                    dve.wait_ge(bias_added, T.b_units(u + 1))
                    nc.vector.tensor_scalar(out=neg_max[:, at:at + 1], in0=top_score[:, 0:1], scalar1=-1.0,
                                            scalar2=None, op0=ALU.mult).then_inc(max_done, 1)
                    return
                reach(dve, exp_done, T("v", u - 3))
                nc.vector.tensor_reduce(neg_max[:, at:at + 1], scores, AX_X, ALU.max, negate=True).then_inc(max_done, 1)

            def invert_sum(T, u):
                dve.wait_ge(exp_done, T("v", u + 1))
                reach(dve, rd_done, T("v", u - 3))
                nc.vector.reciprocal(rden[:, u % 4:u % 4 + 1], den[:, u % 4:u % 4 + 1]).then_inc(rd_own, 1)
                dve.wait_ge(rd_own, T("v", u + 1))
                reach(dve, t_ready, T("v2", 2 * u - 2))
                nc.vector.tensor_scalar(out=DG[:, u % 2, :], in0=con("ident"), scalar1=rden[:, u % 4:u % 4 + 1],
                                        scalar2=None, op0=ALU.mult).then_inc(rd_done, 1)

            def probs_lo(T, u, n):
                for g, first, m in banks(n):
                    dve.wait_ge(th_done, T("v2", 2 * u + g + 1))
                    nc.vector.tensor_tensor(probs_t(PTl, u, first, m),
                                            TP[:, g, 0:m * P].rearrange("p (k q) -> p k q", q=P),
                                            probs_t(PTh, u, first, m).bitcast(F32), ALU.subtract).then_inc(tl_done, 1)

            def whole_output(T, g):
                e = g // 2 % 2
                part = slice(e * HD, (e + 1) * HD)
                dve.wait_ge(ot_done, T("vg", g + 1))
                reach(dve, mixed_done, T("vg", g - 1))
                nc.vector.tensor_tensor(OS[part, g % 2, :], OB[0:HD, g % 2, :], OT[0:HD, g % 2, :],
                                        ALU.add).then_inc(os_done, 1)

            def attend(T, kind, i, before, last):
                dve.wait_ge(a_free, T("a"))
                for u in range(PAIR):
                    for w, k in lagged(u, 2, kind, before):
                        invert_sum(T, w)
                    for w, k in lagged(u, 1, kind, before):
                        row_maxima(T, w, k, width(k, w))
                    for w, k in lagged(u, 3, kind, before):
                        probs_lo(T, w, width(k, w))
                    for w, k in lagged(u, 8, kind, before):
                        if w % 4 == 3:
                            whole_output(T, w // 4)

            def attend_end(T):
                invert_sum(T, -2)
                row_maxima(T, -1, "B", width("B", -1))
                probs_lo(T, -3, width("B", -3))
                invert_sum(T, -1)
                for u in (-2, -1):
                    probs_lo(T, u, width("B", u))
                whole_output(T, -2)
                whole_output(T, -1)

            def scale_x(T):
                invert(T, 0)
                for hf in range(NH):
                    dve.wait_ge(rstd_ready, T("n", hf + 1))
                    for k in range(KT):
                        if hf == 0 and k == 4:
                            invert(T, 1)
                        nc.vector.scalar_tensor_tensor(out=X[:, k, half(hf)], in0=X[:, k, half(hf)],
                                                       scalar=col("final2")[:, k:k + 1], in1=(B7, Dn[:, 0, :])[hf],
                                                       op0=ALU.mult, op1=ALU.mult).then_inc(x_scaled, 1)

            walk(dve, dict(start=start, prepare=prepare, ada=ada, mods=mods, split=split,
                           norm_pool=norm_pool, norm=norm, pool=pool, up=up, down=down, spatial=spatial,
                           normalise_v=normalise_v, mix=mix, resplit=resplit, project=project, scale_x=scale_x,
                           heads=heads, vals=vals, plain=plain, attend=attend, attend_end=attend_end))

        @block.tensor
        def _(pe):
            def product(out_bank, hi_lo_w, hi_lo_x, start, stop):
                (whi, wlo), (xhi, xlo) = hi_lo_w, hi_lo_x
                nc.tensor.matmul(out_bank, whi, xhi, start=start, stop=False)
                nc.tensor.matmul(out_bank, whi, xlo, start=False, stop=False)
                return nc.tensor.matmul(out_bank, wlo, xhi, start=False, stop=stop)

            def weights(T, at):
                c = T.n["c"] % 2
                return Whi[:, c, at:at + P], Wlo[:, c, at:at + P]

            def start(T):
                pe.wait_ge(set_ready, 6)

            def ada(T, l, cc, q):
                pass

            def mods(T, l, cc):
                pe.wait_ge(unit_done, T("u"))
                reach(pe, mod_done, T("mod"))
                for j in range(KT):
                    ins = nc.tensor.matmul(B6[:, j:j + 1], acc[:, j * P:(j + 1) * P], ones[:, 0:1],
                                           start=True, stop=True)
                ins.then_inc(ada_sum, 1)

            def stat(T, hf, squares, start, stop, weights=None):
                rhs = ones[:, 0:1] if weights is None else weights
                n = rhs.shape[-1]
                for t in range(4):
                    ins = nc.tensor.matmul(stats(hf)[:, n * t:n * t + n], squares[:, t * P:(t + 1) * P], rhs,
                                           start=start and t == 0, stop=stop and t == 3)
                ins.then_inc(stat_done, 1)

            def first_seven(T, order, hf):
                pe.wait_ge(sum_done, T("s", adds(order, complete(order, hf) - 1)))
                stat(T, hf, sums(order, hf), True, False)

            def eighth(T, order, hf):
                i = complete(order, hf) - 1
                pe.wait_ge(sq_done, T("q", i + 1))
                stat(T, hf, SQ[:, i % 2, :], False, True)

            def both_stats(T, i):
                hf, k = tile("down", i)
                pe.wait_ge(sq_done, T("q", i + 1))
                pe.wait_ge(g_sq_ready, 2)
                stat(T, hf, SQ[:, i % 2, :], k == 0, k == KT - 1, g_sq[:, k, :])

            def spread(T, hf, bank):
                pe.wait_ge(diag_ready, T("n", hf + 1))
                nc.tensor.matmul(bank, ones[:], diag[:], start=True, stop=True).then_inc(rstd_ready, 1)

            def completed(T, i, then):
                if i == 2:
                    reach(pe, mod_done, T("mod"))
                    reach(pe, std_ready, T("n"))
                if then == 4 and i >= 2:
                    both_stats(T, i - 2)
                elif i == 9:
                    first_seven(T, "down", 0)
                elif i == 10:
                    eighth(T, "down", 0)
                if i == 12:
                    reach(pe, tb_ready, T("b"))
                    spread(T, 0, B7)

            def ada_rows(T, cc, q):
                u = 4 * cc + q
                if u == 0:
                    pe.wait_ge(c_ready, 1)
                if q == 0:
                    reach(pe, row_copied, 2 * cc - 2)
                pe.wait_ge(stage_in[u % STAGES], 16 * (u // STAGES + 1))
                for kk in range(2):
                    for h in range(2):
                        ins = nc.tensor.matmul(Dn[0:1, 2 * (cc % 2) + h, :], c_act[:, 2 * q + kk:2 * q + kk + 1],
                                               stage[:, u % STAGES, kk * D + h * H:kk * D + (h + 1) * H],
                                               start=q + kk == 0, stop=q + kk == 4)
                        if q == 3 and kk == 1 and h == 0:
                            ins.then_inc(row_ready, 1)
                ins.then_inc(unit_done, 1)

            def mods0(T, pair):
                pe.wait_ge(row_copied, 4 * pair + 4)
                reach(pe, mod_done, pair)
                for j in range(2 * KT):
                    ins = nc.tensor.matmul(A[:, 0, 2 * KT * pair + j:2 * KT * pair + j + 1],
                                           rows[pair][0:1, j // KT, j % KT * P:(j % KT + 1) * P], ones[0:1, 0:1],
                                           start=True, stop=True)
                ins.then_inc(ada_sum, 1)

            def norm_pool(T):
                for u in range(24):
                    ada_rows(T, u // 4, u % 4)
                    if u in (5, 8):
                        first_seven(T, "down", u // 3 - 1)
                        eighth(T, "down", u // 3 - 1)
                    if u in (6, 9):
                        spread(T, u // 3 - 2, (B7, B6)[u // 3 - 2])
                    if u == 9:
                        mods0(T, 0)
                    if u == 17:
                        mods0(T, 1)

            def norm(T, which, order):
                if which == 4:
                    both_stats(T, 14)
                    both_stats(T, 15)
                else:
                    first_seven(T, order, 1)
                    eighth(T, order, 1)
                if order == "project":
                    pe.wait_ge(tb_ready, T("b"))
                    spread(T, 0, B7)
                spread(T, 1, Dn[:, 0, :])

            def pool(T, then):
                pe.wait_ge(pool_w_split, 1)
                pe.wait_ge(row_copied, 10)
                for hf in range(NH):
                    for k in range(KT):
                        i, g, d = hf * KT + k, k // 2, k % 2
                        reach(pe, d_free, T("d", i - D_BANKS + 1))
                        if i == 2:
                            pe.wait_ge(row_copied, 12)
                        for kk in range(2):
                            pe.wait_ge(lo_done, 2 * g + kk + 1)
                            ins = product(Dn[:, i % D_BANKS, :], weights(T, (2 * g + kk) * 2 * P + d * P),
                                          (Hhi[:, 2 * g + kk, half(hf)], Hlo[:, 2 * g + kk, half(hf)]),
                                          kk == 0, kk == 1)
                        ins.then_inc(d_ready, 1)
                        completed(T, i, then)
                        if i == 5:
                            mods0(T, 2)

            def up(T, par, first=False):
                pe.wait_ge(unit_done, T("uc"))
                for hf in range(NH):
                    for f in range(FT):
                        i = hf * FT + f
                        reach(pe, a_free, T("a", i - A_BANKS + 1))
                        for k in range(KT):
                            if first and f == 0:
                                pe.wait_ge(lo_done, T("h", hf * KT + k + 1 - 2 * KT))
                            ins = product(A[:, i % A_BANKS, :], weights(T, k * UC + f * P),
                                          (Hhi[:, k, half(hf)], Hlo[:, k, half(hf)]), k == 0, k == KT - 1)
                        ins.then_inc(a_ready, 1)

            def down(T, gate, par, ahead, then=None):
                pe.wait_ge(unit_done, T("uc"))
                for hf in range(NH):
                    for k in range(KT):
                        i = hf * KT + k
                        reach(pe, d_free, T("d", i - D_BANKS + 1))
                        for f in range(FT):
                            if i == 0:
                                pe.wait_ge(lo_done, T("h", -ahead))
                            ins = product(Dn[:, i % D_BANKS, :], weights(T, f * D + k * P),
                                          (Mhi[:, par, f, half(hf)], Mlo[:, par, f, half(hf)]), f == 0, f == FT - 1)
                        ins.then_inc(d_ready, 1)
                        if then is not None:
                            completed(T, i, then)

            def spatial(T):
                pe.wait_ge(ws_masked, KT)
                pe.wait_ge(tb_ready, T("b"))
                for g, bank in enumerate((B6, B7)):
                    ins = nc.tensor.matmul(bank, ones[:], ws[:, 4 * g:4 * g + 4, :], start=True, stop=True)
                ins.then_inc(row_sum, 1)

            def values(T, j):
                pe.wait_ge(unit_done, T("uc"))
                c = T.n["c"] % 2
                for i in range(KT):
                    reach(pe, a_free, T("a", i - A_BANKS + 1))
                    for k in range(KT):
                        if j == 0:
                            pe.wait_ge(lo_done, T("h", KT * (i // 4) + k + 1 - 2 * KT))
                        tok = slice(i * P, (i + 1) * P)
                        out_bank, w = A[:, i % A_BANKS, 0:UC], slice(k * UC, (k + 1) * UC)
                        nc.tensor.matmul(out_bank, Hhi[:, k, tok], Whi[:, c, w], start=k == 0, stop=False)
                        nc.tensor.matmul(out_bank, Hhi[:, k, tok], Wlo[:, c, w], start=False, stop=False)
                        ins = nc.tensor.matmul(out_bank, Hlo[:, k, tok], Whi[:, c, w], start=False, stop=k == KT - 1)
                    ins.then_inc(a_ready, 1)

            def mix(T, j):
                for h in range(2):
                    pe.wait_ge(lo_done, T("h", 2 * h - 2))
                    for hf in range(NH):
                        i = 2 * h + hf
                        reach(pe, d_free, T("d", i - D_BANKS + 1))
                        for n in range(4):
                            ins = product(Dn[:, i, n * P:(n + 1) * P], (Vhi[:, h, 4 * hf + n, :], Vlo[:, h, 4 * hf + n, :]),
                                          (WShi[:, h, :], WSlo[:, h, :]), True, True)
                        ins.then_inc(d_ready, 1)

            def first_rstd(hf):
                pe.wait_ge(r1_diag, hf + 1)
                nc.tensor.matmul(A[:, hf, :], ones[:], diag[:], start=True, stop=True).then_inc(r1_ready, 1)

            def project(T, j, gate, first, then=None):
                pe.wait_ge(unit_done, T("uc"))
                for i in range(4):
                    hf, f = i // 2, i % 2
                    if then == 5 and first and f == 0:
                        first_rstd(hf)
                    reach(pe, d_free, T("d", i - D_BANKS + 1))
                    for k in range(KT):
                        if first and f == 0:
                            pe.wait_ge(lo_done, T("h", hf * KT + k + 1 - 2 * KT))
                        ins = product(Dn[:, i, :], weights(T, k * UC + f * P),
                                      (Hhi[:, k, half(hf)], Hlo[:, k, half(hf)]), k == 0, k == KT - 1)
                    ins.then_inc(d_ready, 1)
                    if then is not None and 4 * j + i == 14:
                        reach(pe, std_ready, T("n"))
                        pe.wait_ge(bs_ready, KT)
                        if then == 5:
                            pe.wait_ge(x_rescaled, 2 * KT)
                        first_seven(T, "project", 0)
                    if then is not None and 4 * j + i == 15:
                        eighth(T, "project", 0)

            def scale_x(T):
                first_seven(T, "project", 1)
                eighth(T, "project", 1)
                pe.wait_ge(os_done, T("vg"))
                spread(T, 0, B7)
                spread(T, 1, Dn[:, 0, :])

            def heads(T, what, j, nf):
                pe.wait_ge(unit_done, T("uc"))
                for i in range(2 * nf):
                    hf, f, r = i // nf, i % nf, T.n["r"] + i
                    reach(pe, a_free, T("a", i - A_BANKS + 1))
                    for k in range(KT):
                        if r == 0 or (r == 2):
                            pe.wait_ge(lo_done, T("h", hf * KT + k + 1 - 2 * KT))
                        ins = product(A[:, i % A_BANKS, :], weights(T, k * UC + f * P),
                                      (Hhi[:, k, half(hf)], Hlo[:, k, half(hf)]), k == 0, k == KT - 1)
                    ins.then_inc(a_ready, 1)
                    head_sum(T, r - 1)
                    head_spread(r - 2)
                    rotate(r - 3)
                if what == "k":
                    head_sum(T, r)
                    head_spread(r - 1)
                    rotate(r - 2)
                    head_spread(r)
                    rotate(r - 1)
                    rotate(r)

            def head_sum(T, r):
                if r >= 0:
                    pe.wait_ge(a_free, r + 1 + T.n["a"] - T.n["r"])
                    if r == 0:
                        pe.wait_ge(tb_ready, T("b"))
                    reach(pe, sd_done, r)
                    for t in range(4):
                        ins = nc.tensor.matmul(Dn[:, 0, 2 * t:2 * t + 2], TB[:, r % 2, t * P:(t + 1) * P],
                                               con("pairs")[:, 0:P:HD], start=True, stop=True)
                    ins.then_inc(ss_ready, 1)

            def head_spread(r):
                if r >= 0:
                    pe.wait_ge(hx_done, r + 1)
                    reach(pe, qn_done, r)
                    for t in range(4):
                        ins = nc.tensor.matmul(B6[:, t * P:(t + 1) * P], HX[:, t, :], con("ident"),
                                               start=True, stop=True)
                    ins.then_inc(hs_ready, 1)

            def rotate(r):
                if r >= 0:
                    pe.wait_ge(qn_done, r + 1)
                    reach(pe, rf_done, r)
                    nc.tensor.matmul(B7, con("rot"), QN[:, r % 2, :], start=True, stop=True).then_inc(rot_ready, 1)

            def plain(T, what, head):
                project(T, 0, None, False)

            def v_a(T):
                for hf in range(NH):
                    reach(pe, a_free, T("a", hf - A_BANKS + 1))
                    for k in range(KT):
                        ins = product(A[:, hf, :], weights(T, k * UC + P),
                                      (Hhi[:, k, half(hf)], Hlo[:, k, half(hf)]), k == 0, k == KT - 1)
                    ins.then_inc(a_ready, 1)

            def vals(T, head, at, n):
                pe.wait_ge(unit_done, T("uc"))
                c = T.n["c"] % 2
                for i in range(QT):
                    reach(pe, d_free, T("d", i - D_BANKS + 1))
                    if n == P:
                        pe.wait_ge(a_free, T("a", i // 4 - 1))
                        if i == 0:
                            pe.wait_ge(sd_done, T("r"))
                        nc.tensor.transpose(Dn[:, i % D_BANKS, 0:P], VF[:, i // 4, i % 4 * P:(i % 4 + 1) * P],
                                            con("ident")).then_inc(d_ready, 1)
                        continue
                    tok, bank = slice(i * P, (i + 1) * P), Dn[:, i % D_BANKS, 0:n]
                    for k in range(KT):
                        w = slice(k * UC + at, k * UC + at + n)
                        nc.tensor.matmul(bank, Hhi[:, k, tok], Whi[:, c, w], start=k == 0, stop=False)
                        nc.tensor.matmul(bank, Hhi[:, k, tok], Wlo[:, c, w], start=False, stop=False)
                        ins = nc.tensor.matmul(bank, Hlo[:, k, tok], Whi[:, c, w], start=False, stop=k == KT - 1)
                    ins.then_inc(d_ready, 1)

            def scores(T, u, kind, n, before):
                e, qt = u // QT, u % QT
                k0 = 0 if kind == "A" else neighbourhood(qt)[0] * GRID
                if qt == 0:
                    pe.wait_ge(qk_loaded[e], T.loads(6 * 16))
                if (kind if u >= 2 else before) == "B":
                    pe.wait_ge(bias_added, T.b_units(u - 1))
                else:
                    reach(pe, exp_done, T("v", u - 1))
                for at in range(0, n, H):
                    m = min(H, n - at)
                    bank = SB_[:, 2 * (u % 2) + at // H, 0:m]
                    q = QS[:, e, qt * P:(qt + 1) * P]
                    nc.tensor.matmul(bank, q, KH[:, e, k0 + at:k0 + at + m], start=True, stop=False)
                    ins = nc.tensor.matmul(bank, q, KL[:, e, k0 + at:k0 + at + m], start=False, stop=True)
                ins.then_inc(s_ready, 1)

            def turn(T, u, n):
                pe.wait_ge(rd_done, T("v", u + 1))
                for g, first, m in banks(n):
                    reach(pe, tl_done, T("v2", 2 * u + g - 1))
                    for k in range(m):
                        a = (first + k) * P
                        part = min(P, n - a)
                        ins = nc.tensor.matmul(TP[0:part, g, k * P:(k + 1) * P], PE_[:, u % 2, a:a + part],
                                               DG[:, u % 2, :], start=True, stop=True)
                    ins.then_inc(t_ready, 1)

            def outputs(T, w, kind):
                g, part_of = w // 4, w % 4
                e = g // 2 % 2
                if w % QT == 0:
                    pe.wait_ge(v_loaded[e], T.loads(16))
                if part_of == 0:
                    reach(pe, os_done, T("vg", g - 1))
                if kind == "A":
                    if part_of == 0:
                        pe.wait_ge(tl_done, T("v2", 8 * g + 8))
                    for k in (2 * part_of, 2 * part_of + 1):
                        for x in (PTh, PTl):
                            ins = nc.tensor.matmul(OB[:, g % 2, :], VT[:, e, k, :], x[:, g % 2, k, :],
                                                   start=k == 0 and x is PTh, stop=k == QT - 1 and x is PTl)
                else:
                    pe.wait_ge(tl_done, T("v2", 2 * w + 2))
                    t = part_of
                    first, rows = neighbourhood(w % QT)
                    n = rows * GRID
                    tiles = (n + P - 1) // P
                    for k in range(tiles):
                        part = min(P, n - k * P)
                        for x in (PTh, PTl):
                            ins = nc.tensor.matmul(OB[:, g % 2, t * P:(t + 1) * P],
                                                   VT[0:part, e, first // 2 + k, :],
                                                   x[0:part, g % 2, k, t * P:(t + 1) * P],
                                                   start=k == 0 and x is PTh, stop=k == tiles - 1 and x is PTl)
                if part_of == 3:
                    ins.then_inc(o_ready, 1)

            def attend(T, kind, i, before, last):
                for u in range(PAIR):
                    for w, k in lagged(u, 3, kind, before):
                        turn(T, w, width(k, w))
                    scores(T, u, kind, width(kind, u), before)
                    for w, k in lagged(u, 7, kind, before):
                        outputs(T, w, k)

            def attend_start(T):
                pe.wait_ge(a_free, T("a"))
                pe.wait_ge(d_free, T("d"))

            def attend_end(T):
                for w in range(-7, 0):
                    if w < -4:
                        turn(T, w + 4, width("B", w + 4))
                    outputs(T, w, "B")

            walk(pe, dict(start=start, v_a=v_a, ada=ada, mods=mods, norm_pool=norm_pool, norm=norm,
                          pool=pool, up=up, down=down, spatial=spatial, values=values, gates=up, mix=mix,
                          project=project, scale_x=scale_x, heads=heads, vals=vals,
                          silu=lambda T, j: up(T, 0), plain=plain, attend_start=attend_start,
                          attend=attend, attend_end=attend_end))


def pack_cols(vectors):
    return np.concatenate([np.ascontiguousarray(v.reshape(-1, P).T) for v in vectors], axis=1)


def constants():
    ident = np.eye(P, dtype=np.float32)
    tri = np.triu(np.ones((P, P), np.float32))
    pairs = np.kron(np.eye(2, dtype=np.float32), np.ones((64, 64), np.float32))
    rot = np.zeros((P, P), np.float32)
    for b in range(4):
        for j in range(16):
            rot[32 * b + 16 + j, 32 * b + j] = -1.0
            rot[32 * b + j, 32 * b + 16 + j] = 1.0
    invc = np.zeros((P, 4, 16), np.float32)
    for g, w in enumerate(WINDOWS):
        invc[:, g, :] = 1.0 / np.minimum(np.arange(16, dtype=np.float32) + 1, w)
    return np.concatenate([ident, tri, pairs, rot, invc.reshape(P, 64)], axis=1)


def rope_tables():
    t = np.arange(S)
    inv = np.float32(10000.0) ** (-np.arange(16, dtype=np.float32) * np.float32(2.0 / 32))
    row = (t // GRID).astype(np.float32)[:, None] * inv
    column = (t % GRID).astype(np.float32)[:, None] * inv
    ang = np.concatenate([row, row, column, column] * 2, axis=1).T
    return np.stack([np.cos(ang), np.sin(ang)]).astype(np.float32)


def masks():
    c = np.arange(GRID)
    start = np.clip(c - NKW // 2, 0, GRID - NKW)
    valid = (c[None, :] >= start[:, None]) & (c[None, :] < start[:, None] + NKW)
    full = np.tile(valid[None, :, None, :], (2, 1, 14, 1))
    inner = np.tile(valid[None, :, None, :], (2, 1, 9, 1))
    inner[0, :, 8] = False
    inner[1, :, 0] = False
    both = np.concatenate([full.reshape(P, -1), inner.reshape(P, -1)], axis=1)
    return np.where(both, np.float32(0), np.float32(-1e30))


def kernel(**inputs):
    import concourse.bacc as bacc
    from concourse.bass_utils import run_bass_kernel_spmd

    g = {k: np.asarray(v) for k, v in inputs.items()}
    two = lambda v: np.concatenate([v.reshape(-1), v.reshape(-1)])
    arrays = {
        "x_t": g["x"][0].T,
        "cols": pack_cols([g["c"], g["ada_b"][0], g["ada_b"][1], g["norm_mix_g"][0], g["norm_mix_g"][1],
                           g["norm_mlp_g"][0], g["norm_mlp_g"][1], g["pool_scale"], g["sgu_ln_g"], g["sgu_ln_b"],
                           g["final_g"], g["norm_gain_2"], g["final_norm_gain_2"], two(g["q_norm_a_2"]),
                           two(g["k_norm_a_2"])]),
        "const": constants(),
        "ada_w": g["ada_w"],
        "pool_w": g["pool_w"][0],
        "sgu_in": g["sgu_w_in"][0],
        "sgu_ws": g["sgu_w_s"][0].transpose(0, 2, 1),
        "sgu_bs": g["sgu_b_s"].reshape(1, -1),
        "sgu_out": g["sgu_w_out"][0],
        "w1": g["mlp_w1"],
        "w2": g["mlp_w2"],
        "rope": rope_tables(),
        "mask": masks(),
        "w_in2": g["w_in_2"][0],
        "rpb": np.pad(g["na_rpb_2"][0], ((0, 0), (0, 0), (48, 48))),
        "w_out2": g["w_out_2"][0],
    }
    arrays = {k: np.ascontiguousarray(v) for k, v in arrays.items()}
    nc = bacc.Bacc("TRN2", target_bir_lowering=False, num_devices=1, dynamic_dma_scratch_size=1024)
    args = [nc.dram_tensor(k, v.shape, mybir.dt.from_np(v.dtype), kind="ExternalInput").ap() for k, v in arrays.items()]
    out = nc.dram_tensor("out_t", (D, S), F32, kind="ExternalOutput").ap()
    build(nc, *args, out)
    r = run_bass_kernel_spmd(nc, [arrays], core_ids=[0])
    return np.ascontiguousarray(r.results[0]["out_t"].T)[None]
```
